# Optimizing a Trainium2 kernel written in Bass

```python
import jax, jax.numpy as jnp
from jax import lax
import numpy as np

D_MODEL = 1024
BATCH = 1
SEQ = 512
DEPTH = 1

D_MIX = D_MODEL
A_HEADS = 8
A_HEAD_DIM = 64
A_WIDTH = A_HEADS * A_HEAD_DIM
IDX_HEADS = 8
IDX_DIM = 32
TOPK_MAX = 256
B_HEADS = 8
B_NOPE_DIM = 64
B_ROPE_DIM = 32
B_V_DIM = 64
B_WIDTH = B_HEADS * B_V_DIM
Q_LORA = 256
KV_LORA = 128

ROPE_THETA = 10000.0
Q_BLOCK = 128
DEEPNORM_ALPHA = (2 * DEPTH) ** 0.25
DEEPNORM_BETA = (8 * DEPTH) ** -0.25
LN_EPS = 1e-5
RMS_EPS = 1e-6

IN_SPLITS = (A_WIDTH, A_WIDTH, A_WIDTH, A_WIDTH, IDX_HEADS * IDX_DIM, IDX_DIM, IDX_HEADS,
             Q_LORA, KV_LORA, B_ROPE_DIM, B_WIDTH)
D_IN = sum(IN_SPLITS)

kernel_name = "hymba_dsa_mla_deepnorm_layer"

def _split_cols(h):
    offs = np.cumsum(np.array(IN_SPLITS))[:-1].tolist()
    return jnp.split(h, offs, axis=-1)

def _rope(x, pos):
    d = x.shape[-1]
    inv = ROPE_THETA ** (-jnp.arange(0, d, 2, dtype=jnp.float32) / d)
    ang = pos.astype(jnp.float32)[..., None] * inv
    cos = jnp.cos(ang)[:, :, None, :]
    sin = jnp.sin(ang)[:, :, None, :]
    xf = x.astype(jnp.float32)
    x1, x2 = xf[..., : d // 2], xf[..., d // 2:]
    out = jnp.concatenate([x1 * cos - x2 * sin, x1 * sin + x2 * cos], axis=-1)
    return out.astype(x.dtype)

def _rmsnorm(x, g):
    xf = x.astype(jnp.float32)
    y = xf * lax.rsqrt(jnp.mean(xf * xf, axis=-1, keepdims=True) + RMS_EPS)
    return (y * g.astype(jnp.float32)).astype(x.dtype)

def _layernorm(x, g, b):
    xf = x.astype(jnp.float32)
    mu = jnp.mean(xf, axis=-1, keepdims=True)
    var = jnp.mean(jnp.square(xf - mu), axis=-1, keepdims=True)
    y = (xf - mu) * lax.rsqrt(var + LN_EPS)
    return (y * g.astype(jnp.float32) + b.astype(jnp.float32)).astype(x.dtype)

def _dsa_branch(q, k, v, iq, ik, iw):
    B, S, H, Dh = q.shape
    k_top = min(TOPK_MAX, S // 4)
    n_blocks = S // Q_BLOCK
    key_pos = jnp.arange(S)
    scale = A_HEAD_DIM ** -0.5
    idx_scale = IDX_DIM ** -0.5
    ikf = ik.astype(jnp.float32)
    iwf = iw.astype(jnp.float32) * (IDX_HEADS ** -0.5)

    def block(i):
        t0 = i * Q_BLOCK
        qb = lax.dynamic_slice_in_dim(q, t0, Q_BLOCK, axis=1).astype(jnp.float32)
        iqb = lax.dynamic_slice_in_dim(iq, t0, Q_BLOCK, axis=1).astype(jnp.float32)
        iwb = lax.dynamic_slice_in_dim(iwf, t0, Q_BLOCK, axis=1)
        qpos = t0 + jnp.arange(Q_BLOCK)
        logits = jnp.einsum('bthd,bsd->bths', iqb, ikf) * idx_scale
        score = jnp.einsum('bth,bths->bts', iwb, jax.nn.relu(logits))
        causal = key_pos[None, :] <= qpos[:, None]
        score = jnp.where(causal[None], score, -jnp.inf)
        _, sel = lax.top_k(score, k_top)
        ks = jax.vmap(lambda kb, ib: kb[ib])(k, sel).astype(jnp.float32)
        vs = jax.vmap(lambda vb, ib: vb[ib])(v, sel).astype(jnp.float32)
        att = jnp.einsum('bthd,btkhd->bhtk', qb, ks) * scale
        valid = sel <= qpos[None, :, None]
        att = jnp.where(valid[:, None], att, -jnp.inf)
        p = jax.nn.softmax(att, axis=-1)
        o = jnp.einsum('bhtk,btkhd->bthd', p, vs)
        return o.astype(q.dtype)

    out = lax.map(block, jnp.arange(n_blocks))
    return out.transpose(1, 0, 2, 3, 4).reshape(B, S, H * Dh)

def _mla_branch(c_q, c_kv, k_rope, q_norm_g, w_uq, kv_norm_g, w_ukv, pos):
    B, S, _ = c_q.shape
    q = (_rmsnorm(c_q, q_norm_g) @ w_uq).reshape(B, S, B_HEADS, B_NOPE_DIM + B_ROPE_DIM)
    q_nope, q_pe = q[..., :B_NOPE_DIM], _rope(q[..., B_NOPE_DIM:], pos)
    kv = (_rmsnorm(c_kv, kv_norm_g) @ w_ukv).reshape(B, S, B_HEADS, B_NOPE_DIM + B_V_DIM)
    k_nope = kv[..., :B_NOPE_DIM].astype(jnp.float32)
    v = kv[..., B_NOPE_DIM:].astype(jnp.float32)
    k_pe = _rope(k_rope[:, :, None, :], pos)[:, :, 0, :].astype(jnp.float32)
    scale = (B_NOPE_DIM + B_ROPE_DIM) ** -0.5
    n_blocks = S // Q_BLOCK
    key_pos = jnp.arange(S)

    def block(i):
        t0 = i * Q_BLOCK
        qn = lax.dynamic_slice_in_dim(q_nope, t0, Q_BLOCK, axis=1).astype(jnp.float32)
        qp = lax.dynamic_slice_in_dim(q_pe, t0, Q_BLOCK, axis=1).astype(jnp.float32)
        qpos = t0 + jnp.arange(Q_BLOCK)
        s = (jnp.einsum('bthd,bshd->bhts', qn, k_nope)
             + jnp.einsum('bthr,bsr->bhts', qp, k_pe)) * scale
        causal = key_pos[None, :] <= qpos[:, None]
        s = jnp.where(causal[None, None], s, -jnp.inf)
        p = jax.nn.softmax(s, axis=-1)
        o = jnp.einsum('bhts,bshd->bthd', p, v)
        return o.astype(c_q.dtype)

    out = lax.map(block, jnp.arange(n_blocks))
    return out.transpose(1, 0, 2, 3, 4).reshape(B, S, B_WIDTH)

def setup_inputs(seed: int = 0) -> dict:
    key = jax.random.key(seed)
    ks = jax.random.split(key, 10)
    x = jax.random.normal(ks[0], (BATCH, SEQ, D_MODEL), jnp.float32)
    positions = jnp.broadcast_to(jnp.arange(SEQ, dtype=jnp.int32), (BATCH, SEQ))
    col_scale = jnp.concatenate([
        jnp.ones((2 * A_WIDTH,), jnp.float32),
        jnp.full((A_WIDTH,), DEEPNORM_BETA, jnp.float32),
        jnp.ones((D_IN - 3 * A_WIDTH,), jnp.float32)])
    w_in = jax.random.normal(ks[1], (DEPTH, D_MODEL, D_IN), jnp.float32) * (D_MODEL ** -0.5) * col_scale
    q_norm_g = 1.0 + 0.01 * jax.random.normal(ks[2], (DEPTH, Q_LORA), jnp.float32)
    w_uq = jax.random.normal(ks[3], (DEPTH, Q_LORA, B_HEADS * (B_NOPE_DIM + B_ROPE_DIM)), jnp.float32) * (Q_LORA ** -0.5)
    kv_norm_g = 1.0 + 0.01 * jax.random.normal(ks[4], (DEPTH, KV_LORA), jnp.float32)
    ukv_scale = jnp.concatenate([jnp.ones((B_NOPE_DIM,), jnp.float32),
                                 jnp.full((B_V_DIM,), DEEPNORM_BETA, jnp.float32)])
    w_ukv = (jax.random.normal(ks[5], (DEPTH, KV_LORA, B_HEADS, B_NOPE_DIM + B_V_DIM), jnp.float32)
             * (KV_LORA ** -0.5) * ukv_scale).reshape(DEPTH, KV_LORA, B_HEADS * (B_NOPE_DIM + B_V_DIM))
    w_out = jax.random.normal(ks[6], (DEPTH, D_MIX, D_MODEL), jnp.float32) * (D_MIX ** -0.5) * DEEPNORM_BETA
    ln_g = 1.0 + 0.01 * jax.random.normal(ks[7], (DEPTH, D_MODEL), jnp.float32)
    ln_b = 0.01 * jax.random.normal(ks[8], (DEPTH, D_MODEL), jnp.float32)
    return {"x": x, "positions": positions, "w_in": w_in, "q_norm_g": q_norm_g,
            "w_uq": w_uq, "kv_norm_g": kv_norm_g, "w_ukv": w_ukv, "w_out": w_out,
            "ln_g": ln_g, "ln_b": ln_b}

def reference(x, positions, w_in, q_norm_g, w_uq, kv_norm_g, w_ukv, w_out, ln_g, ln_b):
    B, S, _ = x.shape
    for l in range(DEPTH):
        h = x @ w_in[l]
        (qa, ka, va, ga, iq, ik, iw, c_q, c_kv, k_rope, gb) = _split_cols(h)
        qa = _rope(qa.reshape(B, S, A_HEADS, A_HEAD_DIM), positions)
        ka = _rope(ka.reshape(B, S, A_HEADS, A_HEAD_DIM), positions)
        va = va.reshape(B, S, A_HEADS, A_HEAD_DIM)
        iq = _rope(iq.reshape(B, S, IDX_HEADS, IDX_DIM), positions)
        ik = _rope(ik[:, :, None, :], positions)[:, :, 0, :]
        o_a = _dsa_branch(qa, ka, va, iq, ik, iw) * jax.nn.silu(ga)
        o_b = _mla_branch(c_q, c_kv, k_rope, q_norm_g[l], w_uq[l], kv_norm_g[l],
                          w_ukv[l], positions) * jax.nn.silu(gb)
        out = jnp.concatenate([o_a, o_b], axis=-1) @ w_out[l]
        x = _layernorm(DEEPNORM_ALPHA * x + out, ln_g[l], ln_b[l])
    return x


_drawn_inputs = setup_inputs


def setup_inputs(seed=0):
    import zlib

    import numpy as np

    out = dict(_drawn_inputs(seed))
    spreads = {}
    factors = {'q_norm_g': 8.0, 'w_uq': 3.33, 'kv_norm_g': 8.0, 'ln_g': 5.73, 'ln_b': 5.982}
    for name, (base, spread) in spreads.items():
        noise = np.random.default_rng([zlib.crc32(name.encode()), seed]).standard_normal(out[name].shape)
        drawn = base * np.exp(spread * noise) if base else spread * noise
        out[name] = __import__('jax').numpy.asarray(drawn.astype(out[name].dtype))
    for name, factor in factors.items():
        out[name] = (out[name] * factor).astype(out[name].dtype)
    return out
```

```python
import numpy as np
import concourse.bass as bass
from concourse import mybir
from contextlib import ExitStack

P = 128
SEQ, D_MODEL = 512, 1024
TT = SEQ // P
KT = D_MODEL // P
A_HEADS, A_DIM = 8, 64
A_WIDTH = A_HEADS * A_DIM
IDX_HEADS, IDX_DIM = 8, 32
TOP_K = min(256, SEQ // 4)
B_HEADS, NOPE, ROPE_D, V_DIM = 8, 64, 32, 64
B_QK = NOPE + ROPE_D
Q_LORA, KV_LORA = 256, 128
QL_T = Q_LORA // P
ALPHA = 2 ** 0.25
LN_EPS, RMS_EPS = 1e-5, 1e-6
BANK = 512
FREQ_A, FREQ_B = A_DIM // 2, ROPE_D // 2
NFREQ = FREQ_A + FREQ_B
NEG = -3.0e38
TAKEN = -3.3e38


def build(nc, x, xT, positions, freqs, w_in, q_norm_g, w_uq, kv_norm_g, w_ukv, w_out, ln_g, ln_b, out):
    f32, f32r, i32 = mybir.dt.float32, mybir.dt.float32r, mybir.dt.int32
    ACT, ALU = mybir.ActivationFunctionType, mybir.AluOpType

    c0 = 4 * A_WIDTH
    N_IDX = IDX_HEADS * IDX_DIM + IDX_DIM + IDX_HEADS
    N_LAT = Q_LORA + KV_LORA + ROPE_D
    GROUPS = [(c0, N_IDX), (c0 + N_IDX, N_LAT), (0, BANK), (A_WIDTH, BANK), (2 * A_WIDTH, BANK),
              (3 * A_WIDTH, BANK), (c0 + N_IDX + N_LAT, BANK)]
    G_IDX, G_LAT, G_Q, G_K, G_V, G_GA, G_GB = range(7)
    NG = len(GROUPS)

    w_in_v = w_in.rearrange("(k p) c -> p k c", p=P)
    w_uq_v = w_uq.rearrange("(k p) c -> p k c", p=P)
    w_ukv_v = w_ukv.rearrange("p (s c) -> p s c", s=2)
    w_out_v = w_out.rearrange("(k p) (s c) -> p k s c", p=P, s=2)
    LOADS = [(w_in_v[:, 2 * q:2 * q + 2, c:c + n], n) for c, n in GROUPS for q in range(KT // 2)]
    C_UQN = 2 * len(LOADS)
    LOADS.append((w_uq_v[:, :, 0:B_HEADS * NOPE], B_HEADS * NOPE))
    C_UQP = 2 * len(LOADS)
    LOADS.append((w_uq_v[:, :, B_HEADS * NOPE:B_HEADS * B_QK], B_HEADS * ROPE_D))
    C_UKN = 2 * len(LOADS)
    C_UKV = C_UKN + 1
    LOADS.append((w_ukv_v, BANK))
    C_OUT = 2 * len(LOADS)
    LOADS += [(w_out_v[:, k], BANK) for k in range(KT)]
    NCHUNK = 2 * len(LOADS)
    RING = 8
    RPAIR = RING // 2

    def width(c):
        return LOADS[c // 2][1]

    ORDER = [3, 2, 1, 0]
    HEADS = A_HEADS + B_HEADS
    NU = TT * HEADS

    def unit(u):
        m, h = ORDER[u // HEADS], u % HEADS
        return m, h, (m + 1) * P

    base = -(-nc.sbuf_base // 64) * 64

    def sb(name, kib, shape, dt=f32):
        return nc.alloc_sbuf_tensor_at(name, shape, dt, offset=base + int(kib * 1024))

    x_hi = sb("x_hi", 0, [P, KT, SEQ], f32r)
    x_lo = sb("x_lo", 16, [P, KT, SEQ], f32r)
    wo_lo = sb("wo_lo", 0, [P, KT, 2, BANK], f32r)
    w_hi = sb("w_hi", 32, [P, RING, BANK], f32r)
    w_lo = sb("w_lo", 48, [P, RING, BANK], f32r)
    wo_hi = sb("wo_hi", 32, [P, KT, 2, BANK], f32r)
    w_raw = sb("w_raw", 64, [P, RING, BANK])
    x_res = sb("x_res", 64, [P, 2, D_MODEL])
    lng = sb("lng", 72, [P, D_MODEL])
    lnb = sb("lnb", 76, [P, D_MODEL])
    iqT = sb("iqT", 80, [P, IDX_HEADS, SEQ - P], f32r)
    ikT = sb("ikT", 92, [P, SEQ], f32r)
    latT_hi = sb("latT_hi", 80, [P, QL_T + 1, SEQ], f32r)
    latT_lo = sb("latT_lo", 86, [P, QL_T + 1, SEQ], f32r)
    oT_hi = sb("oT_hi", 80, [P, KT, P], f32r)
    oT_lo = sb("oT_lo", 84, [P, KT, P], f32r)
    o_sb = sb("o_sb", 88, [P, D_MODEL])
    tmp = sb("tmp", 94, [P, 2, BANK])
    y = sb("y", 94, [P, D_MODEL])
    x_raw = sb("x_raw", 98, [P, KT, SEQ])
    iq_st = sb("iq_st", 98, [P, TT - 1, IDX_HEADS, 4, IDX_DIM])
    ik_st = sb("ik_st", 110, [P, TT, 4, IDX_DIM])
    qbT = sb("qbT", 98, [B_QK, B_HEADS, SEQ])
    q_tok = sb("q_tok", 114, [P, TT, A_WIDTH])
    k_tok = sb("k_tok", 122, [P, TT, A_WIDTH])
    kbT = sb("kbT", 114, [B_QK, B_HEADS, SEQ])
    relu = sb("relu", 130, [P, 4, BANK])
    vb = sb("vb", 130, [P, TT, B_HEADS * V_DIM])
    idx_tok = sb("idx_tok", 138, [P, TT, N_IDX])
    lat_tok = sb("lat_tok", 143, [P, TT, N_LAT])
    gate = sb("gate", 138, [P, TT, D_MODEL])
    va = sb("va", 154, [P, TT, A_WIDTH])
    qaT = sb("qaT", 162, [P, A_HEADS // 2, SEQ])
    kaT = sb("kaT", 170, [P, A_HEADS // 2, SEQ])
    qpe_tok = sb("qpe_tok", 178, [P, TT, B_HEADS * ROPE_D])
    probs = sb("probs", 178, [P, 4, BANK])
    trig_tmp = sb("trig_tmp", 186, [P, 3, 2 * TT * NFREQ])
    probsT = sb("probsT", 186, [P, 3, BANK])
    causal = sb("causal", 192, [P, SEQ])
    score = sb("score", 194, [P, (2 + 3 + 4) * P])
    trig = sb("trig", 198.5, [P, 2, TT, NFREQ])
    ident = sb("ident", 200, [P, P])
    kpe_tok = sb("kpe_tok", 200.5, [P, TT, ROPE_D])
    small = sb("small", 201, [P, 256])
    pos_i = sb("pos_i", 202, [P, TT], i32)
    freq_sb = sb("freq_sb", 202.25, [P, NFREQ])

    SCORE_AT = {1: 0, 2: 2 * P, 3: 5 * P}
    at = 0

    def col(n):
        nonlocal at
        at += n
        return small[:, at - n:at]

    pos_f, iw = col(TT), col(TT * IDX_HEADS)
    ssq, lat_r = col(2 * TT), col(2 * TT)
    gq, gkv = col(QL_T), col(1)
    top8 = col(8 * (TT - 1))
    neg_max, row_sum, rinv = col(8), col(NU), col(HEADS)
    stats, aggr, rstd = col(12), col(3), col(1)
    minus_half = col(2 * TT)

    with ExitStack() as ctx:
        ps = ctx.enter_context(nc.psum_tensor("ps", [P, 8, BANK], f32))
        acc, side = ps[:, 0:4], ps[:, 4:8]
        ps_s, ps_pT, ps_o, ps_y = ps[:, 0:2], ps[:, 2:4], ps[:, 4:6], ps[:, 6:8]

        def sem(name):
            return ctx.enter_context(nc.semaphore(name))

        x_loaded = [sem(f"x_loaded{i}") for i in range(KT // 2)]
        w_loaded = [sem(f"w_loaded{i}") for i in range(RPAIR)]
        pos_loaded, norm_g_loaded, ln_loaded = sem("pos_loaded"), sem("norm_g_loaded"), sem("ln_loaded")
        xres_loaded = [sem(f"xres_loaded{i}") for i in range(2)]
        stored = sem("stored")
        kpe_copied = sem("kpe_copied")
        const_ready = sem("const_ready")
        x_hi_ready, x_lo_ready = sem("x_hi_ready"), sem("x_lo_ready")
        w_hi_ready, w_lo_ready = sem("w_hi_ready"), sem("w_lo_ready")
        chunk_used = sem("chunk_used")
        acc_ready = sem("acc_ready")
        side_ready = sem("side_ready")
        acc_free = [sem(f"acc_free{i}") for i in range(4)]
        side_free = [sem(f"side_free{i}") for i in range(4)]
        tok_ready = sem("tok_ready")
        trig_arg_ready, trig_ready = sem("trig_arg_ready"), sem("trig_ready")
        idx_split = sem("idx_split")
        relu_ready, relu_used = sem("relu_ready"), sem("relu_used")
        lat_normed, lat_hi_ready, lat_lo_ready = sem("lat_normed"), sem("lat_hi_ready"), sem("lat_lo_ready")
        lat_ms_ready, lat_rs_ready = sem("lat_ms_ready"), sem("lat_rs_ready")
        var_ready, rstd_ready = sem("var_ready"), sem("rstd_ready")
        idxT_ready = sem("idxT_ready")
        qk_rotated = sem("qk_rotated")
        kpe_rotated, qpe_rotated, qpe_tok_ready = sem("kpe_rotated"), sem("qpe_rotated"), sem("qpe_tok_ready")
        a_kt_ready, a_qt_ready = sem("a_kt_ready"), sem("a_qt_ready")
        kpeT_ready = sem("kpeT_ready")
        b_act_ready, b_dve_ready = sem("b_act_ready"), sem("b_dve_ready")
        vb_ready = sem("vb_ready")
        bias_ready = sem("bias_ready")
        scores_ready, masked_ready, probs_ready = sem("scores_ready"), sem("masked_ready"), sem("probs_ready")
        probsT_ready, probsT_copied = sem("probsT_ready"), sem("probsT_copied")
        pv_done = sem("pv_done")
        o_ps_read, o_ready, oT_ps_ready = sem("o_ps_read"), sem("o_ready"), sem("oT_ps_ready")
        oT_hi_ready, oT_lo_ready = sem("oT_hi_ready"), sem("oT_lo_ready")
        out_ps_ready, out_ps_read, y_ready = sem("out_ps_ready"), sem("out_ps_read"), sem("y_ready")
        dve_step = sem("dve_step")

        block = ctx.enter_context(nc.Block())

        F_IQ, F_IK = 0, 2 * (TT - 1)
        F_LOGIT = F_IK + 1
        F_LAT = F_LOGIT + (TT - 1) * IDX_HEADS
        F_QT = F_LAT + QL_T + 1
        F_KT = F_QT + A_HEADS // 2
        F_QPE = F_KT + A_HEADS // 2
        F_QPET = F_QPE + TT
        F_KPET = F_QPET + 2
        F_END = F_KPET + 1
        A_QN = NG * TT
        A_KN = A_QN + 4
        A_VB = A_KN + 4
        A_END = A_VB + TT

        def free_at(n):
            return 2 * (n // 4)

        @block.sync
        def _(sp):
            def load(q):
                if q >= RPAIR:
                    sp.wait_ge(w_lo_ready, 2 * (q - RPAIR) + 2)
                src, n = LOADS[q]
                s = 2 * (q % RPAIR)
                sp.dma_start(w_raw[:, s:s + 2, 0:n], src).then_inc(w_loaded[q % RPAIR], 16)

            xT_v = xT.rearrange("(k p) t -> p k t", p=P)
            for q in range(KT // 2):
                sp.dma_start(x_raw[:, 2 * q:2 * q + 2, :], xT_v[:, 2 * q:2 * q + 2, :]).then_inc(x_loaded[q], 16)
                load(q)
                if q == 0:
                    sp.dma_start(pos_i[:, :], positions).then_inc(pos_loaded, 16)
                    sp.dma_start(freq_sb[:, :], freqs).then_inc(pos_loaded, 16)
            sp.dma_start(gq, q_norm_g).then_inc(norm_g_loaded, 16)
            sp.dma_start(gkv, kv_norm_g).then_inc(norm_g_loaded, 16)
            for q in range(RPAIR, len(LOADS)):
                load(q)
                if q == C_OUT // 2 + 1:
                    sp.wait_ge(kpeT_ready, 1)
                    sp.dma_start(kbT[NOPE:B_QK, 1:B_HEADS, :],
                                 kbT[NOPE:B_QK, 0:1, :].broadcast_to([ROPE_D, B_HEADS - 1, SEQ])).then_inc(kpe_copied, 16)
            sp.wait_ge(w_lo_ready, NCHUNK)
            sp.dma_start(lng[:, :], ln_g.broadcast_to([P, D_MODEL])).then_inc(ln_loaded, 16)
            sp.dma_start(lnb[:, :], ln_b.broadcast_to([P, D_MODEL])).then_inc(ln_loaded, 16)
            for i, m in enumerate(ORDER):
                if i < 2:
                    sp.dma_start(x_res[:, i % 2, :], x[m * P:(m + 1) * P, :]).then_inc(xres_loaded[i % 2], 16)
            for i, m in enumerate(ORDER):
                sp.wait_ge(y_ready, i + 1)
                sp.dma_start(out[m * P:(m + 1) * P, :], y[:, :]).then_inc(stored, 16)
                if i + 2 < TT:
                    m2 = ORDER[i + 2]
                    sp.dma_start(x_res[:, i % 2, :], x[m2 * P:(m2 + 1) * P, :]).then_inc(xres_loaded[i % 2], 16)
            sp.wait_ge(stored, 16 * TT)

        @block.gpsimd
        def _(pool):
            pool.memset(causal[:, :], 0.0).then_inc(const_ready, 1)
            pool.memset(ident[:, :], 0.0).then_inc(const_ready, 1)
            pool.memset(minus_half, -0.5).then_inc(const_ready, 1)
            pool.wait_ge(const_ready, 3)
            pool.affine_select(out=causal[:, :], in_=causal[:, :], compare_op=ALU.is_ge, fill=NEG,
                               base=SEQ - P, pattern=[[-1, SEQ]], channel_multiplier=1).then_inc(const_ready, 1)
            pool.affine_select(out=ident[:, :], in_=ident[:, :], compare_op=ALU.not_equal, fill=1.0,
                               base=0, pattern=[[-1, P]], channel_multiplier=1).then_inc(const_ready, 1)
            for c in range(NCHUNK):
                n, s = width(c), c % RING
                pool.wait_ge(w_loaded[(c // 2) % RPAIR], 16 * (c // 2 // RPAIR + 1))
                pool.wait_ge(w_hi_ready, c + 1)
                if c < C_OUT:
                    dst, hi = w_lo[:, s, 0:n], w_hi[:, s, 0:n]
                else:
                    k, half = divmod(c - C_OUT, 2)
                    dst, hi = wo_lo[:, k, half], wo_hi[:, k, half]
                pool.tensor_tensor(dst, w_raw[:, s, 0:n], hi, ALU.subtract).then_inc(w_lo_ready, 1)
                if c == KT * (G_Q + 1) - 1:
                    pool.wait_ge(const_ready, 5)
                    pool.wait_ge(lat_ms_ready, 1)
                    pool.tensor_tensor(lat_r, lat_r, minus_half, ALU.pow).then_inc(lat_rs_ready, 1)
            for i in range(TT):
                pool.wait_ge(var_ready, i + 1)
                pool.tensor_tensor(rstd, aggr[:, 2:3], minus_half[:, 0:1], ALU.pow).then_inc(rstd_ready, 1)

        @block.scalar
        def _(act):
            def split_hi(c):
                n, s = width(c), c % RING
                act.wait_ge(w_loaded[(c // 2) % RPAIR], 16 * (c // 2 // RPAIR + 1))
                if c >= C_OUT:
                    k, half = divmod(c - C_OUT, 2)
                    dst = wo_hi[:, k, half]
                    act.wait_ge(acc_ready, A_END)
                else:
                    dst = w_hi[:, s, 0:n]
                    if c >= RING:
                        g, k = divmod(c - RING, KT)
                        if k < KT - 1:
                            act.wait_ge(chunk_used, (KT - 1) * g + k + 1)
                        else:
                            act.wait_ge(acc_ready, TT * (g + 1))
                act.activation(dst, w_raw[:, s, 0:n], ACT.Copy).then_inc(w_hi_ready, 1)

            def evac_group(g):
                dst = {G_IDX: idx_tok, G_LAT: lat_tok, G_Q: q_tok, G_K: k_tok, G_V: va}.get(g, gate)
                off = A_WIDTH if g == G_GB else 0
                n = GROUPS[g][1]
                if g == G_GA:
                    act.wait_ge(relu_used, (TT - 1) * IDX_HEADS)
                    act.wait_ge(kpe_rotated, 1)
                    act.wait_ge(side_ready, F_LAT + QL_T + 1)
                for m in range(TT):
                    act.wait_ge(acc_ready, TT * g + m + 1)
                    act.activation(dst[:, m, off:off + n], acc[:, m, 0:n],
                                   ACT.Silu if g in (G_GA, G_GB) else ACT.Copy).then_inc(acc_free[m], 2)
                    act.wait_ge(acc_free[m], 2 * (g + 1))
                act.sem_inc(tok_ready, 1)

            for k in range(KT):
                act.wait_ge(x_loaded[k // 2], 16)
                act.activation(x_hi[:, k, :], x_raw[:, k, :], ACT.Copy).then_inc(x_hi_ready, 1)
                split_hi(k)
            act.wait_ge(trig_arg_ready, 1)
            act.activation(trig[:, :, :, :].rearrange("p a t f -> p (a t f)"), trig_tmp[:, 0, :], ACT.Sin).then_inc(trig_ready, 1)

            def evac_idxT():
                for n in range(F_LOGIT):
                    act.wait_ge(side_ready, n + 1)
                    if n < F_IK:
                        m, quad = divmod(n, 2)
                        dst = iqT[:, 4 * quad:4 * quad + 4, m * P:(m + 1) * P]
                    else:
                        dst = ikT[:, :].rearrange("p (a b) -> p a b", a=4)
                    act.activation(dst, side[:, n % 4].rearrange("p (a b) -> p a b", a=4), ACT.Copy).then_inc(side_free[n % 4], 2)
                    act.wait_ge(side_free[n % 4], free_at(n) + 2)
                act.sem_inc(idxT_ready, 1)

            def relu_unit(i):
                m, h = 1 + i // IDX_HEADS, i % IDX_HEADS
                n, N = F_LOGIT + i, (m + 1) * P
                act.wait_ge(side_ready, n + 1)
                if i >= 4:
                    act.wait_ge(relu_used, i - 3)
                act.activation(relu[:, i % 4, 0:N], side[:, n % 4, 0:N], ACT.Relu, scale=IDX_DIM ** -0.5).then_inc(side_free[n % 4], 2)
                act.wait_ge(side_free[n % 4], free_at(n) + 2)
                act.sem_inc(relu_ready, 1)

            def evac_lat_hi():
                act.wait_ge(norm_g_loaded, 32)
                for t in range(QL_T + 1):
                    n = F_LAT + t
                    act.wait_ge(side_ready, n + 1)
                    act.activation(latT_hi[:, t, :], side[:, n % 4], ACT.Copy,
                                   scale=gq[:, t:t + 1] if t < QL_T else gkv).then_inc(lat_hi_ready, 1)

            for g in range(NG):
                first = KT * (g + 1)
                if g == G_LAT:
                    for c in range(first, first + KT - 1):
                        split_hi(c)
                    evac_group(g)
                    evac_idxT()
                    split_hi(first + KT - 1)
                elif g == G_Q:
                    for j in range(KT):
                        if j < KT - 1:
                            split_hi(first + j)
                        for i in range(3 * j, 3 * j + 3):
                            relu_unit(i)
                    evac_group(g)
                    split_hi(first + KT - 1)
                elif g < NG - 1:
                    for c in range(first, first + KT - 1):
                        split_hi(c)
                    evac_group(g)
                    if g == G_V:
                        evac_lat_hi()
                    split_hi(first + KT - 1)
                else:
                    for c in range(C_UQN, C_OUT):
                        split_hi(c)
                    evac_group(g)

            for p in range(4):
                n = A_QN + p
                act.wait_ge(acc_ready, n + 1)
                act.activation(qbT[0:NOPE, 2 * p, :], acc[0:NOPE, p], ACT.Copy).then_inc(acc_free[p], 1)
            for p in range(4):
                n = F_QT + p
                act.wait_ge(side_ready, n + 1)
                act.activation(qaT[:, p, :], side[:, n % 4], ACT.Copy).then_inc(side_free[n % 4], 2)
                act.wait_ge(side_free[n % 4], free_at(n) + 2)
            act.sem_inc(a_qt_ready, 1)
            for m in range(TT):
                n = F_QPE + m
                act.wait_ge(side_ready, n + 1)
                act.activation(qpe_tok[:, m, :], side[:, n % 4, 0:B_HEADS * ROPE_D], ACT.Copy).then_inc(side_free[n % 4], 2)
                act.wait_ge(side_free[n % 4], free_at(n) + 2)
                act.sem_inc(qpe_tok_ready, 1)
            for p in range(4):
                n = A_KN + p
                act.wait_ge(acc_ready, n + 1)
                act.activation(kbT[0:NOPE, 2 * p, :], acc[0:NOPE, p], ACT.Copy).then_inc(acc_free[p], 1)
            for m in range(TT):
                n = A_VB + m
                act.wait_ge(acc_ready, n + 1)
                act.activation(vb[:, m, :], acc[:, m], ACT.Copy).then_inc(acc_free[m], 2)
                act.wait_ge(acc_free[m], free_at(n) + 2)
            act.sem_inc(vb_ready, 1)
            for quad in range(2):
                n = F_QPET + quad
                act.wait_ge(side_ready, n + 1)
                for j in range(2):
                    a = act.activation(qbT[NOPE:B_QK, 4 * quad + j, :], side[32 * j:32 * j + 32, n % 4], ACT.Copy)
                a.then_inc(side_free[n % 4], 1)
            n = F_KPET
            act.wait_ge(side_ready, n + 1)
            act.activation(kbT[NOPE:B_QK, 0, :], side[0:ROPE_D, n % 4], ACT.Copy).then_inc(kpeT_ready, 1)
            act.wait_ge(kpeT_ready, 1)
            act.sem_inc(side_free[n % 4], 2)
            act.sem_inc(b_act_ready, 1)

            def exp_unit(u):
                m, h, N = unit(u)
                act.wait_ge(masked_ready, u + 1)
                act.activation(probs[:, u % 4, 0:N], probs[:, u % 4, 0:N], ACT.Exp, bias=neg_max[:, u % 8:u % 8 + 1],
                               scale=-1.0, accum_out=row_sum[:, u:u + 1]).then_inc(probs_ready, 1)

            def copy_probsT(u):
                N = unit(u)[2]
                act.wait_ge(probsT_ready, u + 1)
                if u >= 3:
                    act.wait_ge(pv_done, u - 2)
                act.activation(probsT[:, u % 3, 0:N], ps_pT[:, u % 2, 0:N], ACT.Copy).then_inc(probsT_copied, 1)

            def copy_oT_hi(i):
                for b in range(2):
                    act.wait_ge(oT_ps_ready, 2 * i + b + 1)
                    if b == 0 and i > 0:
                        act.wait_ge(out_ps_ready, 2 * i)
                    act.activation(oT_hi[:, 4 * b:4 * b + 4, :], ps_y[:, b].rearrange("p (a b) -> p a b", a=4),
                                   ACT.Copy).then_inc(oT_hi_ready, 1)

            nc_out = 0
            for u in range(NU + T_LAG):
                if u < NU:
                    exp_unit(u)
                if u >= T_LAG:
                    copy_probsT(u - T_LAG)
                if nc_out < 2 * KT:
                    for _ in range(2):
                        split_hi(C_OUT + nc_out)
                        nc_out += 1
                if u >= HEADS and u % HEADS == OT_AT:
                    copy_oT_hi(u // HEADS - 1)
            copy_oT_hi(TT - 1)

        @block.vector
        def _(dve):
            count = [0]

            def step(ins):
                ins.then_inc(dve_step, 1)
                count[0] += 1
                return count[0]

            def after(ins):
                dve.wait_ge(dve_step, step(ins))

            V = nc.vector

            for k in range(KT):
                dve.wait_ge(x_loaded[k // 2], 16)
                dve.wait_ge(x_hi_ready, k + 1)
                V.tensor_tensor(x_lo[:, k, :], x_raw[:, k, :], x_hi[:, k, :], ALU.subtract).then_inc(x_lo_ready, 1)

            nt = TT * NFREQ
            ang, turns = trig_tmp[:, 0, :], trig_tmp[:, 1, :]
            ROUND = 1.5 * 2 ** 23
            two_pi = 2 * np.pi
            C1 = 6.28125
            C2 = float(np.round((two_pi - C1) * 2 ** 20) / 2 ** 20)
            C3 = float(two_pi - C1 - C2)
            dve.wait_ge(pos_loaded, 32)
            after(V.tensor_copy(pos_f, pos_i[:, :]))
            for half in range(2):
                dst = ang[:, half * nt:(half + 1) * nt].rearrange("p (t f) -> p t f", t=TT)
                last = step(V.tensor_tensor(dst, pos_f.unsqueeze(2).broadcast_to([P, TT, NFREQ]),
                                            freq_sb[:, :].unsqueeze(1).broadcast_to([P, TT, NFREQ]), ALU.mult))
            dve.wait_ge(dve_step, last)
            for half in range(2):
                s = slice(half * nt, (half + 1) * nt)
                last = step(V.tensor_scalar(turns[:, s], ang[:, s], float(1 / two_pi), 0.25 * half, ALU.mult, ALU.add))
            dve.wait_ge(dve_step, last)
            after(V.tensor_scalar(turns, turns, ROUND, ROUND, ALU.add, ALU.subtract))
            for c in (C1, C2, C3):
                after(V.scalar_tensor_tensor(out=ang, in0=turns, scalar=-c, in1=ang, op0=ALU.mult, op1=ALU.add))
            after(V.tensor_scalar(ang[:, nt:], ang[:, nt:], float(np.pi / 2), None, ALU.add))
            V.tensor_scalar(ang, ang, 3.1415925, -3.1415925, ALU.min, ALU.max).then_inc(trig_arg_ready, 1)

            def rope(dst, src, m, heads, half, f0, wait=None):
                n = heads * 2 * half
                s4 = src.rearrange("p (h a f) -> p h a f", a=2, f=half)
                d4 = dst.rearrange("p (h a f) -> p h a f", a=2, f=half)
                t1 = tmp[:, 0, 0:n].rearrange("p (h a f) -> p h a f", a=2, f=half)
                t2 = tmp[:, 1, 0:n].rearrange("p (h a f) -> p h a f", a=2, f=half)
                cos = trig[:, 1, m, f0:f0 + half].unsqueeze(1).broadcast_to([P, heads, half])
                sin = trig[:, 0, m, f0:f0 + half].unsqueeze(1).broadcast_to([P, heads, half])
                for a in range(2):
                    step(V.tensor_tensor(t1[:, :, a], s4[:, :, a], cos, ALU.mult))
                    last = step(V.tensor_tensor(t2[:, :, a], s4[:, :, 1 - a], sin, ALU.mult))
                dve.wait_ge(dve_step, last)
                step(V.tensor_tensor(d4[:, :, 0], t1[:, :, 0], t2[:, :, 0], ALU.subtract))
                after(V.tensor_tensor(d4[:, :, 1], t1[:, :, 1], t2[:, :, 1], ALU.add))

            nrot = (IDX_HEADS + 1) * IDX_DIM
            dve.wait_ge(trig_ready, 1)
            dve.wait_ge(tok_ready, G_IDX + 1)
            step(V.tensor_scalar(iw.rearrange("p (t h) -> p t h", t=TT), idx_tok[:, :, nrot:N_IDX],
                                 IDX_HEADS ** -0.5, None, ALU.mult))
            for m in range(TT):
                rope(idx_tok[:, m, 0:nrot], idx_tok[:, m, 0:nrot], m, IDX_HEADS + 1, FREQ_B, FREQ_A)
                q3 = idx_tok[:, m, 0:IDX_HEADS * IDX_DIM].rearrange("p (h d) -> p h d", d=IDX_DIM)
                k2 = idx_tok[:, m, IDX_HEADS * IDX_DIM:nrot]
                k3 = k2.unsqueeze(1).broadcast_to([P, 2, IDX_DIM])
                if m > 0:
                    st = iq_st[:, m - 1]
                    for a in (0, 2):
                        last = step(V.tensor_copy(st[:, :, a].bitcast(f32r), q3))
                kst = ik_st[:, m]
                last = step(V.tensor_copy(kst[:, 0:2].bitcast(f32r), k3))
                dve.wait_ge(dve_step, last)
                if m > 0:
                    for a in (1, 3):
                        last = step(V.tensor_tensor(st[:, :, a].bitcast(f32r), q3, st[:, :, 0], ALU.subtract))
                V.tensor_tensor(kst[:, 2:4].bitcast(f32r), k3, kst[:, 0:2], ALU.subtract).then_inc(idx_split, 1)

            dve.wait_ge(tok_ready, G_LAT + 1)
            dve.wait_ge(idx_split, TT)
            for m in range(TT):
                for j, (a, b) in enumerate(((0, Q_LORA), (Q_LORA, Q_LORA + KV_LORA))):
                    src = lat_tok[:, m, a:b]
                    last = step(V.tensor_tensor_reduce(out=tmp[:, m % 2, a:b], in0=src, in1=src, scale=1.0, scalar=0.0,
                                                       op0=ALU.mult, op1=ALU.add, accum_out=ssq[:, 2 * m + j:2 * m + j + 1]))
                dve.wait_ge(dve_step, last)
            ssq2, lat_r2 = (v.rearrange("p (t j) -> p t j", j=2) for v in (ssq, lat_r))
            for j, n in enumerate((Q_LORA, KV_LORA)):
                last = step(V.tensor_scalar(lat_r2[:, :, j], ssq2[:, :, j], 1.0 / n, RMS_EPS, ALU.mult, ALU.add))
            dve.wait_ge(dve_step, last)
            dve.sem_inc(lat_ms_ready, 1)
            dve.wait_ge(lat_rs_ready, 1)
            for m in range(TT):
                for j, (a, b) in enumerate(((0, Q_LORA), (Q_LORA, Q_LORA + KV_LORA))):
                    last = V.tensor_scalar(lat_tok[:, m, a:b], lat_tok[:, m, a:b], lat_r[:, 2 * m + j:2 * m + j + 1],
                                           None, ALU.mult).then_inc(lat_normed, 1)
            for m in range(TT):
                rope(kpe_tok[:, m, :], lat_tok[:, m, Q_LORA + KV_LORA:N_LAT], m, 1, FREQ_B, FREQ_A)
            dve.sem_inc(kpe_rotated, 1)

            dve.wait_ge(const_ready, 5)
            for i in range((TT - 1) * IDX_HEADS):
                m, h = 1 + i // IDX_HEADS, i % IDX_HEADS
                N = (m + 1) * P
                sc = score[:, SCORE_AT[m]:SCORE_AT[m] + N]
                dve.wait_ge(relu_ready, i + 1)
                if h > 0:
                    dve.wait_ge(relu_used, i)
                V.scalar_tensor_tensor(out=sc, in0=relu[:, i % 4, 0:N], scalar=iw[:, m * IDX_HEADS + h:m * IDX_HEADS + h + 1],
                                       in1=causal[:, SEQ - N:SEQ] if h == 0 else sc, op0=ALU.mult,
                                       op1=ALU.add).then_inc(relu_used, 1)
            dve.wait_ge(relu_used, (TT - 1) * IDX_HEADS)

            def rope_qk(g):
                dve.wait_ge(tok_ready, g + 1)
                src = q_tok if g == G_Q else k_tok
                for m in range(TT):
                    rope(src[:, m, :], src[:, m, :], m, A_HEADS, FREQ_A, 0)
                dve.sem_inc(qk_rotated, 1)

            spans = [score[:, SCORE_AT[m]:SCORE_AT[m] + (m + 1) * P] for m in range(1, TT)]
            for r in range(TOP_K // 8):
                for j, sc in enumerate(spans):
                    if r > 0:
                        dve.wait_ge(dve_step, count[0] - 2)
                    step(V.max(top8[:, 8 * j:8 * j + 8], sc))
                for j, sc in enumerate(spans):
                    dve.wait_ge(dve_step, count[0] - 2)
                    step(V.match_replace(out=sc, in_to_replace=top8[:, 8 * j:8 * j + 8], in_values=sc, imm_value=TAKEN))
            dve.wait_ge(dve_step, count[0])
            V.tensor_scalar(score[:, :], score[:, :], TAKEN, NEG, ALU.not_equal, ALU.mult).then_inc(bias_ready, 1)

            rope_qk(G_Q)
            rope_qk(G_K)

            for t in range(QL_T + 1):
                n = F_LAT + t
                dve.wait_ge(lat_hi_ready, t + 1)
                V.scalar_tensor_tensor(out=latT_lo[:, t, :], in0=side[:, n % 4], scalar=gq[:, t:t + 1] if t < QL_T else gkv,
                                       in1=latT_hi[:, t, :], op0=ALU.mult, op1=ALU.subtract).then_inc(side_free[n % 4], 2)
                dve.wait_ge(side_free[n % 4], free_at(n) + 2)
            dve.sem_inc(lat_lo_ready, 1)

            for p in range(4):
                dve.wait_ge(acc_ready, A_QN + p + 1)
                V.tensor_copy(qbT[0:NOPE, 2 * p + 1, :], acc[NOPE:P, p]).then_inc(acc_free[p], 1)
            for p in range(4):
                n = F_KT + p
                dve.wait_ge(side_ready, n + 1)
                V.tensor_copy(kaT[:, p, :], side[:, n % 4]).then_inc(side_free[n % 4], 2)
                dve.wait_ge(side_free[n % 4], free_at(n) + 2)
            dve.sem_inc(a_kt_ready, 1)
            for m in range(TT):
                dve.wait_ge(qpe_tok_ready, m + 1)
                rope(qpe_tok[:, m, :], qpe_tok[:, m, :], m, B_HEADS, FREQ_B, FREQ_A)
            dve.sem_inc(qpe_rotated, 1)
            for p in range(4):
                dve.wait_ge(acc_ready, A_KN + p + 1)
                V.tensor_copy(kbT[0:NOPE, 2 * p + 1, :], acc[NOPE:P, p]).then_inc(acc_free[p], 1)
            for quad in range(2):
                n = F_QPET + quad
                dve.wait_ge(side_ready, n + 1)
                for j in range(2, 4):
                    a = V.tensor_copy(qbT[NOPE:B_QK, 4 * quad + j, :], side[32 * j:32 * j + 32, n % 4])
                a.then_inc(side_free[n % 4], 1)
                dve.wait_ge(side_free[n % 4], free_at(n) + 2)
            dve.sem_inc(b_dve_ready, 1)

            def mask_unit(u):
                m, h, N = unit(u)
                a = h < A_HEADS
                bias = spans[m - 1] if a and m > 0 else causal[:, SEQ - N:SEQ]
                scale = (A_DIM if a else B_QK) ** -0.5
                dve.wait_ge(scores_ready, u + 1)
                if u >= 4:
                    dve.wait_ge(probsT_ready, u - 3)
                V.tensor_tensor_reduce(out=probs[:, u % 4, 0:N], in0=ps_s[:, u % 2, 0:N], in1=bias, scale=-scale, scalar=3.0e38,
                                       op0=ALU.add, op1=ALU.min, accum_out=neg_max[:, u % 8:u % 8 + 1]).then_inc(masked_ready, 1)

            def normalise(i, br):
                m = ORDER[i]
                u0 = HEADS * i + A_HEADS * br
                cols = slice(A_WIDTH * br, A_WIDTH * (br + 1))
                dve.wait_ge(pv_done, u0 + A_HEADS)
                r = rinv[:, A_HEADS * br:A_HEADS * (br + 1)]
                after(V.reciprocal(r, row_sum[:, u0:u0 + A_HEADS]))
                if br == 0 and i > 0:
                    dve.wait_ge(oT_ps_ready, 2 * i)
                V.tensor_tensor(o_sb[:, cols].rearrange("p (h d) -> p h d", h=A_HEADS),
                                ps_o[:, br].rearrange("p (h d) -> p h d", h=A_HEADS),
                                r.unsqueeze(2).broadcast_to([P, A_HEADS, A_DIM]), ALU.mult).then_inc(o_ps_read, 1)
                dve.wait_ge(o_ps_read, 2 * i + br + 1)
                V.tensor_tensor(o_sb[:, cols], o_sb[:, cols], gate[:, m, cols], ALU.mult).then_inc(o_ready, 1)

            def copy_oT_lo(i):
                for b in range(2):
                    dve.wait_ge(oT_hi_ready, 2 * i + b + 1)
                    V.tensor_tensor(oT_lo[:, 4 * b:4 * b + 4, :], ps_y[:, b].rearrange("p (a b) -> p a b", a=4),
                                    oT_hi[:, 4 * b:4 * b + 4, :], ALU.subtract).then_inc(oT_lo_ready, 1)

            def layer_norm(i):
                dve.wait_ge(xres_loaded[i % 2], 16 * (i // 2 + 1))
                if i == 0:
                    dve.wait_ge(ln_loaded, 32)
                else:
                    dve.wait_ge(stored, 16 * i)
                for b in range(2):
                    cols = slice(BANK * b, BANK * (b + 1))
                    dve.wait_ge(out_ps_ready, 2 * i + b + 1)
                    V.scalar_tensor_tensor(out=y[:, cols], in0=x_res[:, i % 2, cols], scalar=ALPHA, in1=ps_y[:, b],
                                           op0=ALU.mult, op1=ALU.add).then_inc(out_ps_read, 1)
                    dve.wait_ge(out_ps_read, 2 * i + b + 1)
                    last = step(V.bn_stats(stats[:, 6 * b:6 * b + 6], y[:, cols]))
                dve.wait_ge(dve_step, last)
                after(V.bn_aggr(aggr[:, 0:2], stats))
                after(V.tensor_scalar(aggr[:, 2:3], aggr[:, 1:2], LN_EPS, None, ALU.add))
                dve.sem_inc(var_ready, 1)
                dve.wait_ge(rstd_ready, i + 1)
                after(V.tensor_scalar(y[:, :], y[:, :], aggr[:, 0:1], rstd, ALU.subtract, ALU.mult))
                after(V.tensor_tensor(y[:, :], y[:, :], lng[:, :], ALU.mult))
                V.tensor_tensor(y[:, :], y[:, :], lnb[:, :], ALU.add).then_inc(y_ready, 1)

            for u in range(NU):
                mask_unit(u)
                i, j = divmod(u, HEADS)
                if i > 0:
                    if j == PV_LAG:
                        normalise(i - 1, 1)
                    if j == OT_AT:
                        copy_oT_lo(i - 1)
                    if j == 0 and i > 1:
                        layer_norm(i - 2)
                if j == A_HEADS + PV_LAG:
                    normalise(i, 0)
            layer_norm(TT - 2)
            normalise(TT - 1, 1)
            copy_oT_lo(TT - 1)
            layer_norm(TT - 1)

        @block.tensor
        def _(pe):
            mm = nc.tensor.matmul

            def products(dst, pairs, start, stop):
                for j, (a, b) in enumerate(pairs):
                    ins = mm(dst, a, b, start=start and j == 0, stop=stop and j == len(pairs) - 1)
                return ins

            def group(g, beside=None):
                n = GROUPS[g][1]
                for k in range(KT):
                    c = KT * g + k
                    s = c % RING
                    if g == 0:
                        pe.wait_ge(x_hi_ready, k + 1)
                        pe.wait_ge(x_lo_ready, k + 1)
                    pe.wait_ge(w_hi_ready, c + 1)
                    pe.wait_ge(w_lo_ready, c + 1)
                    for m in range(TT):
                        if k == 0 and g > 0:
                            pe.wait_ge(acc_free[m], 2 * g)
                        t = slice(m * P, (m + 1) * P)
                        wh, wl = w_hi[:, s, 0:n], w_lo[:, s, 0:n]
                        ins = products(acc[:, m, 0:n], ((x_hi[:, k, t], wh), (x_hi[:, k, t], wl), (x_lo[:, k, t], wh)),
                                       k == 0, k == KT - 1)
                        if k == KT - 1:
                            ins.then_inc(acc_ready, 1)
                        elif m == TT - 1:
                            ins.then_inc(chunk_used, 1)
                    if beside:
                        beside(k)

            def fill(n):
                if n >= 4:
                    pe.wait_ge(side_free[n % 4], free_at(n))
                return side[:, n % 4]

            def idx_transposes():
                pe.wait_ge(idx_split, TT)
                pe.wait_ge(const_ready, 5)
                for n in range(F_LOGIT):
                    bank = fill(n)
                    for j in range(4):
                        if n < F_IK:
                            m, quad = divmod(n, 2)
                            src = iq_st[:, m, 4 * quad + j].rearrange("p a d -> p (a d)")
                        else:
                            src = ik_st[:, j].rearrange("p a d -> p (a d)")
                        ins = nc.tensor.transpose(bank[:, j * P:(j + 1) * P], src, ident[:, :])
                    ins.then_inc(side_ready, 1)

            def idx_logits(k):
                if k == 0:
                    pe.wait_ge(idxT_ready, 1)
                for i in range(3 * k, 3 * k + 3):
                    m, h = 1 + i // IDX_HEADS, i % IDX_HEADS
                    N = (m + 1) * P
                    bank = fill(F_LOGIT + i)
                    mm(bank[:, 0:N], iqT[:, h, (m - 1) * P:m * P], ikT[:, 0:N], start=True, stop=True).then_inc(side_ready, 1)

            def lat_transposes():
                pe.wait_ge(lat_normed, 2 * TT)
                for t in range(QL_T + 1):
                    bank = fill(F_LAT + t)
                    for m in range(TT):
                        ins = nc.tensor.transpose(bank[:, m * P:(m + 1) * P], lat_tok[:, m, t * P:(t + 1) * P], ident[:, :])
                    ins.then_inc(side_ready, 1)

            for g in range(NG):
                group(g, idx_logits if g == G_Q else None)
                if g == G_LAT:
                    idx_transposes()
                if g == G_V:
                    lat_transposes()

            def wait_chunk(c):
                pe.wait_ge(w_hi_ready, c + 1)
                pe.wait_ge(w_lo_ready, c + 1)

            pe.wait_ge(lat_hi_ready, QL_T + 1)
            pe.wait_ge(lat_lo_ready, 1)
            wait_chunk(C_UQN + 1)
            for p in range(4):
                pe.wait_ge(acc_free[p], free_at(A_QN + p))
                for t in range(QL_T):
                    s = (C_UQN + t) % RING
                    cols = slice(p * P, (p + 1) * P)
                    ins = products(acc[:, p], ((w_hi[:, s, cols], latT_hi[:, t, :]), (w_hi[:, s, cols], latT_lo[:, t, :]),
                                               (w_lo[:, s, cols], latT_hi[:, t, :])), t == 0, t == QL_T - 1)
                ins.then_inc(acc_ready, 1)
            wait_chunk(C_UQP + 1)
            npe = B_HEADS * ROPE_D

            def qpe():
                for m in range(TT):
                    bank = fill(F_QPE + m)
                    t0 = slice(m * P, (m + 1) * P)
                    for t in range(QL_T):
                        s = (C_UQP + t) % RING
                        ins = products(bank[:, 0:npe], ((latT_hi[:, t, t0], w_hi[:, s, 0:npe]), (latT_hi[:, t, t0], w_lo[:, s, 0:npe]),
                                                        (latT_lo[:, t, t0], w_hi[:, s, 0:npe])), t == 0, t == QL_T - 1)
                    ins.then_inc(side_ready, 1)

            def a_transposes():
                for f0, src in ((F_QT, q_tok), (F_KT, k_tok)):
                    pe.wait_ge(qk_rotated, 1 if src is q_tok else 2)
                    for p in range(4):
                        bank = fill(f0 + p)
                        for m in range(TT):
                            ins = nc.tensor.transpose(bank[:, m * P:(m + 1) * P], src[:, m, p * P:(p + 1) * P], ident[:, :])
                        ins.then_inc(side_ready, 1)

            a_transposes()
            qpe()
            wait_chunk(C_UKV)
            for p in range(4):
                pe.wait_ge(acc_free[p], free_at(A_KN + p))
                s, cols = C_UKN % RING, slice(p * P, (p + 1) * P)
                products(acc[:, p], ((w_hi[:, s, cols], latT_hi[:, QL_T, :]), (w_hi[:, s, cols], latT_lo[:, QL_T, :]),
                                     (w_lo[:, s, cols], latT_hi[:, QL_T, :])), True, True).then_inc(acc_ready, 1)
            for m in range(TT):
                pe.wait_ge(acc_free[m], free_at(A_VB + m))
                s, t0 = C_UKV % RING, slice(m * P, (m + 1) * P)
                ins = products(acc[:, m], ((latT_hi[:, QL_T, t0], w_hi[:, s, :]), (latT_hi[:, QL_T, t0], w_lo[:, s, :]),
                                           (latT_lo[:, QL_T, t0], w_hi[:, s, :])), True, True).then_inc(acc_ready, 1)
            pe.wait_ge(qpe_rotated, 1)
            for quad in range(2):
                bank = fill(F_QPET + quad)
                for m in range(TT):
                    ins = nc.tensor.transpose(bank[:, m * P:(m + 1) * P], qpe_tok[:, m, quad * P:(quad + 1) * P], ident[:, :])
                ins.then_inc(side_ready, 1)
            pe.wait_ge(kpe_rotated, 1)
            bank = fill(F_KPET)
            for m in range(TT):
                ins = nc.tensor.transpose(bank[0:ROPE_D, m * P:(m + 1) * P], kpe_tok[:, m, :], ident[:, :])
            ins.then_inc(side_ready, 1)

            def scores(u):
                m, h, N = unit(u)
                b = u % 2
                if u < 2:
                    pe.wait_ge(acc_free[b], free_at(A_END + b))
                else:
                    pe.wait_ge(masked_ready, u - 1)
                t = slice(m * P, (m + 1) * P)
                if h < A_HEADS:
                    rows, p = slice(A_DIM * (h % 2), A_DIM * (h % 2) + A_DIM), h // 2
                    if u == 0:
                        pe.wait_ge(a_qt_ready, 1)
                        pe.wait_ge(a_kt_ready, 1)
                    q, k = qaT[rows, p, t], kaT[rows, p, 0:N]
                else:
                    if u == A_HEADS:
                        pe.wait_ge(b_act_ready, 1)
                        pe.wait_ge(b_dve_ready, 1)
                        pe.wait_ge(kpe_copied, 16)
                    q, k = qbT[:, h - A_HEADS, t], kbT[:, h - A_HEADS, 0:N]
                mm(ps_s[:, b, 0:N], q, k, start=True, stop=True).then_inc(scores_ready, 1)

            def transposes(u):
                m, h, N = unit(u)
                b = u % 2
                if u < 2:
                    pe.wait_ge(acc_free[2 + b], free_at(A_END + 2 + b))
                else:
                    pe.wait_ge(probsT_copied, u - 1)
                pe.wait_ge(probs_ready, u + 1)
                for j in range(m + 1):
                    ins = nc.tensor.transpose(ps_pT[:, b, j * P:(j + 1) * P], probs[:, u % 4, j * P:(j + 1) * P], ident[:, :])
                ins.then_inc(probsT_ready, 1)

            def outputs(u):
                m, h, N = unit(u)
                br, hh = divmod(h, A_HEADS)
                i = u // HEADS
                if hh == 0:
                    if i == 0:
                        last = [n for n in range(F_END) if n % 4 == br][-1]
                        pe.wait_ge(side_free[br], free_at(last) + 2)
                        if br == 1:
                            pe.wait_ge(vb_ready, 1)
                        else:
                            pe.wait_ge(tok_ready, G_GB + 1)
                    else:
                        pe.wait_ge(o_ps_read, 2 * (i - 1) + br + 1)
                pe.wait_ge(probsT_copied, u + 1)
                v = va if br == 0 else vb
                for j in range(m + 1):
                    ins = mm(ps_o[:, br, hh * A_DIM:(hh + 1) * A_DIM], probsT[:, u % 3, j * P:(j + 1) * P],
                             v[:, j, hh * A_DIM:(hh + 1) * A_DIM], start=(j == 0), stop=(j == m))
                ins.then_inc(pv_done, 1)

            def o_transposes(i):
                pe.wait_ge(o_ready, 2 * i + 2)
                for b in range(2):
                    if i == 0:
                        last = [n for n in range(F_END) if n % 4 == 2 + b][-1]
                        pe.wait_ge(side_free[2 + b], free_at(last) + 2)
                    else:
                        pe.wait_ge(out_ps_read, 2 * i - 1 + b)
                    for j in range(4):
                        ins = nc.tensor.transpose(ps_y[:, b, j * P:(j + 1) * P], o_sb[:, (4 * b + j) * P:(4 * b + j + 1) * P], ident[:, :])
                    ins.then_inc(oT_ps_ready, 1)

            def out_products(i, a, z):
                for n in range(a, z):
                    b, r = divmod(n, 3 * KT)
                    k, j = divmod(r, 3)
                    if n == 0:
                        pe.wait_ge(oT_hi_ready, 2 * i + 2)
                        pe.wait_ge(oT_lo_ready, 2 * i + 2)
                        if i == 0:
                            pe.wait_ge(w_lo_ready, NCHUNK)
                    o, w = ((oT_hi, wo_hi), (oT_hi, wo_lo), (oT_lo, wo_hi))[j]
                    ins = mm(ps_y[:, b], o[:, k, :], w[:, k, b], start=(r == 0), stop=(r == 3 * KT - 1))
                    if r == 3 * KT - 1:
                        ins.then_inc(out_ps_ready, 1)

            per = -(-6 * KT // (HEADS - OUT_AT))
            for u in range(NU + PV_LAG):
                if u < NU:
                    scores(u)
                if 0 <= u - T_LAG < NU:
                    transposes(u - T_LAG)
                if u - PV_LAG >= 0:
                    outputs(u - PV_LAG)
                i, j = divmod(u, HEADS)
                if 0 < i < TT:
                    if j == OT_AT:
                        o_transposes(i - 1)
                    if j >= OUT_AT:
                        out_products(i - 1, per * (j - OUT_AT), min(per * (j - OUT_AT + 1), 6 * KT))
            o_transposes(TT - 1)
            out_products(TT - 1, 0, 6 * KT)


T_LAG, PV_LAG = 2, 3
OT_AT, OUT_AT = 5, 7


def kernel(**inputs):
    import concourse.bacc as bacc
    from concourse.bass_utils import run_bass_kernel_spmd

    nc = bacc.Bacc("TRN2", target_bir_lowering=False, num_devices=1)
    a = {n: np.asarray(v) for n, v in inputs.items()}
    uq = a["w_uq"][0].reshape(Q_LORA, B_HEADS, B_QK)
    ukv = a["w_ukv"][0].reshape(KV_LORA, B_HEADS, NOPE + V_DIM)

    def parts(w, n):
        return np.concatenate([w[:, :, :n].reshape(w.shape[0], -1), w[:, :, n:].reshape(w.shape[0], -1)], axis=1)

    freqs = np.concatenate([np.float32(10000.0) ** (-np.arange(0, d, 2, dtype=np.float32) / np.float32(d))
                            for d in (A_DIM, ROPE_D)]).astype(np.float32)
    arrays = {
        "x": a["x"][0],
        "xT": a["x"][0].T,
        "positions": a["positions"][0].reshape(TT, P).T,
        "freqs": np.tile(freqs, (P, 1)),
        "w_in": a["w_in"][0],
        "q_norm_g": a["q_norm_g"][0].reshape(QL_T, P).T,
        "w_uq": parts(uq, NOPE),
        "kv_norm_g": a["kv_norm_g"][0].reshape(1, P).T,
        "w_ukv": parts(ukv, NOPE),
        "w_out": a["w_out"][0],
        "ln_g": a["ln_g"],
        "ln_b": a["ln_b"],
    }
    arrays = {n: np.ascontiguousarray(v) for n, v in arrays.items()}
    aps = {n: nc.dram_tensor(f"in_{n}", v.shape, mybir.dt.from_np(v.dtype), kind="ExternalInput").ap()
           for n, v in arrays.items()}
    out = nc.dram_tensor("out_y", (SEQ, D_MODEL), mybir.dt.float32, kind="ExternalOutput").ap()
    build(nc, out=out, **aps)
    r = run_bass_kernel_spmd(nc, [{f"in_{n}": v for n, v in arrays.items()}], core_ids=[0])
    return r.results[0]["out_y"].reshape(1, SEQ, D_MODEL)
```

```python
import numpy as np
import concourse.bass as bass
from concourse import mybir
from contextlib import ExitStack

P = 128
SEQ, D_MODEL = 512, 1024
TT = SEQ // P
KT = D_MODEL // P
A_HEADS, A_DIM = 8, 64
A_WIDTH = A_HEADS * A_DIM
IDX_HEADS, IDX_DIM = 8, 32
TOP_K = min(256, SEQ // 4)
B_HEADS, NOPE, ROPE_D, V_DIM = 8, 64, 32, 64
B_QK = NOPE + ROPE_D
Q_LORA, KV_LORA = 256, 128
QL_T = Q_LORA // P
ALPHA = 2 ** 0.25
LN_EPS, RMS_EPS = 1e-5, 1e-6
BANK = 512
FREQ_A, FREQ_B = A_DIM // 2, ROPE_D // 2
NFREQ = FREQ_A + FREQ_B
NEG = -3.0e38
TAKEN = -3.3e38


def build(nc, x, xT, positions, freqs, w_in, q_norm_g, w_uq, kv_norm_g, w_ukv, w_out, ln_g, ln_b, out):
    f32, f32r, i32 = mybir.dt.float32, mybir.dt.float32r, mybir.dt.int32
    ACT, ALU = mybir.ActivationFunctionType, mybir.AluOpType

    c0 = 4 * A_WIDTH
    N_IDX = IDX_HEADS * IDX_DIM + IDX_DIM + IDX_HEADS
    N_LAT = Q_LORA + KV_LORA + ROPE_D
    GROUPS = [(c0, N_IDX), (c0 + N_IDX, N_LAT), (0, BANK), (A_WIDTH, BANK), (2 * A_WIDTH, BANK),
              (3 * A_WIDTH, BANK), (c0 + N_IDX + N_LAT, BANK)]
    G_IDX, G_LAT, G_Q, G_K, G_V, G_GA, G_GB = range(7)
    NG = len(GROUPS)

    w_in_v = w_in.rearrange("(k p) c -> p k c", p=P)
    w_uq_v = w_uq.rearrange("(k p) c -> p k c", p=P)
    w_ukv_v = w_ukv.rearrange("p (s c) -> p s c", s=2)
    w_out_v = w_out.rearrange("(k p) (s c) -> p k s c", p=P, s=2)
    LOADS = [(w_in_v[:, 2 * q:2 * q + 2, c:c + n], n) for c, n in GROUPS for q in range(KT // 2)]
    C_UQN = 2 * len(LOADS)
    LOADS.append((w_uq_v[:, :, 0:B_HEADS * NOPE], B_HEADS * NOPE))
    C_UQP = 2 * len(LOADS)
    LOADS.append((w_uq_v[:, :, B_HEADS * NOPE:B_HEADS * B_QK], B_HEADS * ROPE_D))
    C_UKN = 2 * len(LOADS)
    C_UKV = C_UKN + 1
    LOADS.append((w_ukv_v, BANK))
    C_OUT = 2 * len(LOADS)
    LOADS += [(w_out_v[:, k], BANK) for k in range(KT)]
    NCHUNK = 2 * len(LOADS)
    RING = 8
    RPAIR = RING // 2

    def width(c):
        return LOADS[c // 2][1]

    ORDER = [3, 2, 1, 0]
    HEADS = A_HEADS
    NU_A = TT * HEADS
    NU = 2 * NU_A
    NPASS = 2 * TT

    def unit(u):
        v, h = divmod(u, HEADS)
        m = ORDER[v % TT]
        return v, m, h, (m + 1) * P

    O_AFTER = [NU_A + HEADS * (i + 1) + OT_AT - T_LAG for i in range(TT - 1)] + [NU]
    slots = []
    for u in range(NU + 1):
        if u < NU:
            slots.append(u)
        for i in range(TT):
            for b in range(2):
                if u == O_AFTER[i] + b * (i < TT - 1):
                    slots.append((i, b))
    OUT_AT = [NU_A + HEADS * (i + 1) + OT_AT + 2 for i in range(TT)]
    slot_of = {x: n for n, x in enumerate(slots)}

    base = -(-nc.sbuf_base // 64) * 64

    def sb(name, kib, shape, dt=f32):
        return nc.alloc_sbuf_tensor_at(name, shape, dt, offset=base + int(kib * 1024))

    x_hi = sb("x_hi", 0, [P, KT, SEQ], f32r)
    x_lo = sb("x_lo", 16, [P, KT, SEQ], f32r)
    qbT = sb("qbT", 0, [B_QK, B_HEADS, SEQ])
    kaT_swap = sb("kaT_swap", 16, [P, A_HEADS, SEQ], f32r)
    wo_lo_a = sb("wo_lo_a", 16, [P, KT // 2, 2, BANK], f32r)
    w_hi = sb("w_hi", 32, [P, RING, BANK], f32r)
    w_lo = sb("w_lo", 48, [P, RING, BANK], f32r)
    wo_hi = sb("wo_hi", 32, [P, KT, 2, BANK], f32r)
    w_raw = sb("w_raw", 64, [P, RING, BANK])
    qpe_tok = sb("qpe_tok", 76, [P, TT, B_HEADS * ROPE_D])
    x_res = sb("x_res", 64, [P, 2, D_MODEL])
    lng = sb("lng", 72, [P, D_MODEL])
    lnb = sb("lnb", 76, [P, D_MODEL])
    iqT = sb("iqT", 80, [P, IDX_HEADS, SEQ - P], f32r)
    ikT = sb("ikT", 92, [P, SEQ], f32r)
    latT_hi = sb("latT_hi", 80, [P, QL_T + 1, SEQ], f32r)
    latT_lo = sb("latT_lo", 86, [P, QL_T + 1, SEQ], f32r)
    oT0 = sb("oT0", 80, [P, 2, KT, P], f32r)
    o_norm = sb("o_norm", 92, [P, A_WIDTH])
    tmp = sb("tmp", 94, [P, 2, BANK])
    y = sb("y", 94, [P, D_MODEL])
    x_raw = sb("x_raw", 98, [P, KT, SEQ])
    iq_st = sb("iq_st", 98, [P, TT - 1, IDX_HEADS, 4, IDX_DIM])
    ik_st = sb("ik_st", 110, [P, TT, 4, IDX_DIM])
    q_st = sb("q_st", 98, [P, TT, A_HEADS, 2, A_DIM])
    kaT = sb("kaT", 98, [P, A_HEADS, SEQ], f32r)
    wo_lo_b = sb("wo_lo_b", 98, [P, KT // 2, 2, BANK], f32r)
    q_tok = sb("q_tok", 114, [P, TT, A_WIDTH])
    k_tok = sb("k_tok", 122, [P, TT, A_WIDTH])
    kbT = sb("kbT", 114, [B_QK, B_HEADS, SEQ])
    relu = sb("relu", 130, [P, 4, BANK])
    q_tmp = sb("q_tmp", 130, [P, 2, BANK])
    vb = sb("vb", 130, [P, TT, B_HEADS * V_DIM])
    idx_tok = sb("idx_tok", 138, [P, TT, N_IDX])
    lat_tok = sb("lat_tok", 143, [P, TT, N_LAT])
    gate = sb("gate", 138, [P, TT, D_MODEL])
    warm = sb("warm", 154, [P, P])
    va = sb("va", 154, [P, TT, A_WIDTH])
    qaT = sb("qaT", 162, [P, A_HEADS, SEQ], f32r)
    oT1 = sb("oT1", 162, [P, 2, KT, P], f32r)
    k_st = sb("k_st", 178, [P, TT, A_HEADS, 2, A_DIM])
    probs = sb("probs", 178, [P, NPROBS, BANK])
    trig_tmp = sb("trig_tmp", 178, [P, 2, 2 * TT * NFREQ])
    probsT = sb("probsT", 188, [P, 3, BANK])
    causal = sb("causal", 194, [P, SEQ])
    score = sb("score", 196, [P, (2 + 3 + 4) * P])
    trig = sb("trig", 200.5, [P, 2, TT, NFREQ])
    ident = sb("ident", 202, [P, P])
    kpe_tok = sb("kpe_tok", 202.5, [P, TT, ROPE_D])
    small = sb("small", 203, [P, 256])
    pos_i = sb("pos_i", 204, [P, TT], i32)
    freq_sb = sb("freq_sb", 204.25, [P, NFREQ])

    def wo_lo(k, half):
        return (wo_lo_a if k < KT // 2 else wo_lo_b)[:, k % (KT // 2), half]

    SCORE_AT = {1: 0, 2: 2 * P, 3: 5 * P}
    at = 0

    def col(n):
        nonlocal at
        at += n
        return small[:, at - n:at]

    pos_f, iw = col(TT), col(TT * IDX_HEADS)
    ssq, lat_r = col(2 * TT), col(2 * TT)
    gq, gkv = col(QL_T), col(1)
    top8 = col(8 * (TT - 1))
    neg_max, row_sum, rinv = col(8), col(NU), col(HEADS)
    stats, aggr, rstd = col(12), col(3), col(1)
    minus_half = col(2 * TT)

    with ExitStack() as ctx:
        ps = ctx.enter_context(nc.psum_tensor("ps", [P, 8, BANK], f32))
        acc, side = ps[:, 0:4], ps[:, 4:8]
        ps_o, ps_y, ps_s, ps_pT = ps[:, 0:2], ps[:, 2:4], ps[:, 4:6], ps[:, 6:8]

        def sem(name):
            return ctx.enter_context(nc.semaphore(name))

        x_loaded = [sem(f"x_loaded{i}") for i in range(5)]
        w_loaded = [sem(f"w_loaded{i}") for i in range(RPAIR)]
        pos_loaded, norm_g_loaded, ln_loaded = sem("pos_loaded"), sem("norm_g_loaded"), sem("ln_loaded")
        xres_loaded = [sem(f"xres_loaded{i}") for i in range(2)]
        kaT_swapped, kpe_copied, stored = sem("kaT_swapped"), sem("kpe_copied"), sem("stored")
        const_ready = sem("const_ready")
        x_hi_ready, x_lo_ready = sem("x_hi_ready"), sem("x_lo_ready")
        w_hi_ready, w_lo_ready = sem("w_hi_ready"), sem("w_lo_ready")
        warm_ready = sem("warm_ready")
        wo_hi_ready = sem("wo_hi_ready")
        wo_lo_ready = sem("wo_lo_ready")
        chunk_used = sem("chunk_used")
        acc_ready = sem("acc_ready")
        side_ready = sem("side_ready")
        acc_read = [sem(f"acc_read{i}") for i in range(4)]
        side_read = [sem(f"side_read{i}") for i in range(4)]
        trig_arg_ready, trig_ready = sem("trig_arg_ready"), sem("trig_ready")
        idx_split = sem("idx_split")
        relu_used = sem("relu_used")
        lat_ms_ready, lat_rs_ready = sem("lat_ms_ready"), sem("lat_rs_ready")
        lat_normed, lat_hi_ready = sem("lat_normed"), sem("lat_hi_ready")
        kpe_rotated, qpe_rotated = sem("kpe_rotated"), sem("qpe_rotated")
        q_step, q_rotated = sem("q_step"), sem("q_rotated")
        q_split, k_split = sem("q_split"), sem("k_split")
        bias_ready = sem("bias_ready")
        scores_ready, masked_ready, probs_ready = sem("scores_ready"), sem("masked_ready"), sem("probs_ready")
        transposed, probsT_copied = sem("transposed"), sem("probsT_copied")
        pv_done = sem("pv_done")
        o_ps_read, o_ready = sem("o_ps_read"), sem("o_ready")
        oT_hi_ready, oT_lo_ready = sem("oT_hi_ready"), sem("oT_lo_ready")
        out_ps_ready, out_ps_read, y_ready = sem("out_ps_ready"), sem("out_ps_read"), sem("y_ready")
        var_ready, rstd_ready = sem("var_ready"), sem("rstd_ready")
        dve_step = sem("dve_step")

        block = ctx.enter_context(nc.Block())

        F_IQ, F_IK = 0, 2 * (TT - 1)
        F_LOGIT = F_IK + 1
        F_LAT = F_LOGIT + (TT - 1) * IDX_HEADS
        F_QT = F_LAT + QL_T + 1
        F_KT = F_QT + A_HEADS
        F_END = F_KT + A_HEADS
        A_QPE = NG * TT
        A_QN = A_QPE + TT
        A_KN = A_QN + 4
        A_VB = A_KN + 4
        A_END = A_VB + TT
        A_QPET, A_KPET = A_END + 2, A_END + 6

        def seen(n):
            return 2 * (n // 4)

        def last_seen(fills, bank):
            return seen([n for n in fills if n % 4 == bank][-1]) + 2

        ACC_LAST = [last_seen([*range(A_END), A_QPET, A_QPET + 1, A_KPET], b) for b in range(4)]
        SIDE_LAST = [last_seen(range(F_END), b) for b in range(4)]

        def wait_chunk_used(eng, c):
            g, k = divmod(c, KT)
            if k < KT - 1:
                eng.wait_ge(chunk_used, (KT - 1) * g + k + 1)
            else:
                eng.wait_ge(acc_ready, TT * (g + 1))

        def wait_tok(eng, g, m):
            eng.wait_ge(acc_read[m], 2 * (g + 1))

        def wait_wo_hi(eng, j):
            if j < RING:
                eng.wait_ge(wo_hi_ready, j + 1)
            else:
                eng.wait_ge(w_hi_ready, C_OUT + j - RING + 1)

        @block.sync
        def _(sp):
            def load(q):
                if q >= RPAIR and 2 * q < C_OUT + RING:
                    sp.wait_ge(w_lo_ready, 2 * (q - RPAIR) + 2)
                elif q >= RPAIR:
                    sp.wait_ge(w_lo_ready, C_OUT + q - RPAIR - C_OUT // 2 + 1)
                    sp.wait_ge(wo_lo_ready, q - RPAIR - C_OUT // 2 + 1)
                src, n = LOADS[q]
                s = 2 * (q % RPAIR)
                sp.dma_start(w_raw[:, s:s + 2, 0:n], src).then_inc(w_loaded[q % RPAIR], 16)

            xT_v = xT.rearrange("(k p) t -> p k t", p=P)
            for q, (a, b) in enumerate(((0, 1), (1, 2), (2, 4), (4, 6), (6, 8))):
                sp.dma_start(x_raw[:, a:b, :], xT_v[:, a:b, :]).then_inc(x_loaded[q], 16)
                if q >= 2:
                    load(q - 1)
                if q == 2:
                    sp.dma_start(pos_i[:, :], positions).then_inc(pos_loaded, 16)
                    sp.dma_start(freq_sb[:, :], freqs).then_inc(pos_loaded, 16)
            sp.dma_start(gq, q_norm_g).then_inc(norm_g_loaded, 16)
            sp.dma_start(gkv, kv_norm_g).then_inc(norm_g_loaded, 16)
            for q in range(RPAIR, C_OUT // 2):
                load(q)
            sp.wait_ge(acc_ready, NG * TT)
            for b in range(4):
                sp.wait_ge(side_read[b], SIDE_LAST[b])
            for a in range(2):
                sp.dma_start(kaT_swap[A_DIM * a:A_DIM * (a + 1)].bitcast(f32), kaT[A_DIM * (1 - a):A_DIM * (2 - a)].bitcast(f32)).then_inc(kaT_swapped, 16)
            sp.wait_ge(acc_ready, A_END + 2)
            for q in range(C_OUT // 2, C_OUT // 2 + RPAIR):
                load(q)
            sp.wait_ge(acc_read[2], ACC_LAST[2])
            sp.dma_start(kbT[NOPE:B_QK, 1:B_HEADS, :],
                         kbT[NOPE:B_QK, 0:1, :].broadcast_to([ROPE_D, B_HEADS - 1, SEQ])).then_inc(kpe_copied, 16)
            for q in range(C_OUT // 2 + RPAIR, len(LOADS)):
                load(q)
            sp.wait_ge(w_lo_ready, C_OUT + KT)
            sp.wait_ge(wo_lo_ready, KT)
            sp.dma_start(lng[:, :], ln_g.broadcast_to([P, D_MODEL])).then_inc(ln_loaded, 16)
            sp.dma_start(lnb[:, :], ln_b.broadcast_to([P, D_MODEL])).then_inc(ln_loaded, 16)
            for i in range(2):
                m = ORDER[i]
                sp.dma_start(x_res[:, i, :], x[m * P:(m + 1) * P, :]).then_inc(xres_loaded[i], 16)
            for i, m in enumerate(ORDER):
                for b in range(2):
                    cols = slice(BANK * b, BANK * (b + 1))
                    sp.wait_ge(y_ready, 2 * i + b + 1)
                    sp.dma_start(out[m * P:(m + 1) * P, cols], y[:, cols]).then_inc(stored, 16)
                if i + 2 < TT:
                    m2 = ORDER[i + 2]
                    sp.dma_start(x_res[:, i, :], x[m2 * P:(m2 + 1) * P, :]).then_inc(xres_loaded[i], 16)
            sp.wait_ge(stored, 32 * TT)

        @block.gpsimd
        def _(pool):
            pool.memset(warm[:, :], 0.0).then_inc(warm_ready, 1)
            pool.memset(causal[:, :], 0.0).then_inc(const_ready, 1)
            pool.memset(ident[:, :], 0.0).then_inc(const_ready, 1)
            pool.memset(minus_half, -0.5).then_inc(const_ready, 1)
            pool.wait_ge(const_ready, 3)
            pool.affine_select(out=causal[:, :], in_=causal[:, :], compare_op=ALU.is_ge, fill=NEG,
                               base=SEQ - P, pattern=[[-1, SEQ]], channel_multiplier=1).then_inc(const_ready, 1)
            pool.affine_select(out=ident[:, :], in_=ident[:, :], compare_op=ALU.not_equal, fill=1.0,
                               base=0, pattern=[[-1, P]], channel_multiplier=1).then_inc(const_ready, 1)
            def rotate_queries(m):
                wait_tok(pool, G_Q, m)
                if m == 0:
                    pool.wait_ge(trig_ready, 1)
                    pool.wait_ge(relu_used, (TT - 1) * IDX_HEADS)
                src, t1, t2 = (v.rearrange("p (h a f) -> p h a f", a=2, f=FREQ_A)
                               for v in (q_tok[:, m, :], q_tmp[:, 0, :], q_tmp[:, 1, :]))
                cos, sin = (trig[:, j, m, 0:FREQ_A].unsqueeze(1).broadcast_to([P, A_HEADS, FREQ_A]) for j in (1, 0))
                if m > 0:
                    pool.wait_ge(q_rotated, 2 * m)
                for a in range(2):
                    pool.tensor_tensor(t1[:, :, a], src[:, :, a], cos, ALU.mult).then_inc(q_step, 1)
                    pool.tensor_tensor(t2[:, :, a], src[:, :, 1 - a], sin, ALU.mult).then_inc(q_step, 1)
                pool.wait_ge(q_step, 4 * (m + 1))
                pool.tensor_tensor(src[:, :, 0], t1[:, :, 0], t2[:, :, 0], ALU.subtract).then_inc(q_rotated, 1)
                pool.tensor_tensor(src[:, :, 1], t1[:, :, 1], t2[:, :, 1], ALU.add).then_inc(q_rotated, 1)

            for c in range(C_OUT):
                n, s = width(c), c % RING
                pool.wait_ge(w_loaded[(c // 2) % RPAIR], 16 * (c // 2 // RPAIR + 1))
                pool.wait_ge(w_hi_ready, c + 1)
                pool.tensor_tensor(w_lo[:, s, 0:n], w_raw[:, s, 0:n], w_hi[:, s, 0:n], ALU.subtract).then_inc(w_lo_ready, 1)
                if c == KT * (G_Q + 1) - 1:
                    pool.wait_ge(const_ready, 5)
                    pool.wait_ge(lat_ms_ready, 1)
                    pool.tensor_tensor(lat_r, lat_r, minus_half, ALU.pow).then_inc(lat_rs_ready, 1)
                if c in Q_ROTATE_AT:
                    rotate_queries(Q_ROTATE_AT.index(c))
            for k in range(KT):
                c = C_OUT + 2 * k
                pool.wait_ge(w_loaded[(c // 2) % RPAIR], 16 * (c // 2 // RPAIR + 1))
                wait_wo_hi(pool, c - C_OUT)
                if k == 0:
                    pool.wait_ge(scores_ready, NU_A)
                pool.tensor_tensor(wo_lo(k, 0), w_raw[:, c % RING, :], wo_hi[:, k, 0], ALU.subtract).then_inc(w_lo_ready, 1)
            for i in range(TT):
                pool.wait_ge(var_ready, i + 1)
                pool.tensor_tensor(rstd, aggr[:, 2:3], minus_half[:, 0:1], ALU.pow).then_inc(rstd_ready, 1)

        @block.scalar
        def _(act):
            act.dma_start(w_raw[:, 0:2, 0:N_IDX], LOADS[0][0]).then_inc(w_loaded[0], 16)

            def split_hi(c):
                n, s = width(c), c % RING
                act.wait_ge(w_loaded[(c // 2) % RPAIR], 16 * (c // 2 // RPAIR + 1))
                if c >= C_OUT:
                    k, half = divmod(c - C_OUT, 2)
                    dst = wo_hi[:, k, half]
                else:
                    dst = w_hi[:, s, 0:n]
                    if c >= RING:
                        wait_chunk_used(act, c - RING)
                act.activation(dst, w_raw[:, s, 0:n], ACT.Copy).then_inc(w_hi_ready, 1)

            def evac_group(g):
                dst = {G_IDX: idx_tok, G_LAT: lat_tok, G_Q: q_tok, G_K: k_tok, G_V: va}.get(g, gate)
                off = A_WIDTH if g == G_GB else 0
                n = GROUPS[g][1]
                if g == G_GA:
                    act.wait_ge(relu_used, (TT - 1) * IDX_HEADS)
                    act.wait_ge(kpe_rotated, TT)
                    act.wait_ge(side_ready, F_LAT + QL_T + 1)
                for m in range(TT):
                    act.wait_ge(acc_ready, TT * g + m + 1)
                    act.activation(dst[:, m, off:off + n], acc[:, m, 0:n],
                                   ACT.Silu if g in (G_GA, G_GB) else ACT.Copy).then_inc(acc_read[m], 2)

            for k in range(KT):
                act.wait_ge(x_loaded[k if k < 2 else 1 + k // 2], 16)
                act.activation(x_hi[:, k, :], x_raw[:, k, :], ACT.Copy).then_inc(x_hi_ready, 1)
                split_hi(k)

            def evac_idxT(n):
                act.wait_ge(side_ready, n + 1)
                if n < F_IK:
                    m, quad = divmod(n, 2)
                    dst = iqT[:, 4 * quad:4 * quad + 4, m * P:(m + 1) * P]
                else:
                    dst = ikT[:, :].rearrange("p (a b) -> p a b", a=4)
                act.activation(dst, side[:, n % 4].rearrange("p (a b) -> p a b", a=4), ACT.Copy).then_inc(side_read[n % 4], 2)

            def relu_unit(i):
                n, N = F_LOGIT + i, (2 + i // IDX_HEADS) * P
                act.wait_ge(side_ready, n + 1)
                if i >= 4:
                    act.wait_ge(relu_used, i - 3)
                act.activation(relu[:, i % 4, 0:N], side[:, n % 4, 0:N], ACT.Relu, scale=IDX_DIM ** -0.5).then_inc(side_read[n % 4], 2)

            def evac_lat_hi():
                act.wait_ge(norm_g_loaded, 32)
                for t in range(QL_T + 1):
                    n = F_LAT + t
                    act.wait_ge(side_ready, n + 1)
                    act.activation(latT_hi[:, t, :], side[:, n % 4], ACT.Copy,
                                   scale=gq[:, t:t + 1] if t < QL_T else gkv).then_inc(lat_hi_ready, 1)

            def evac_qT(h):
                n = F_QT + h
                act.wait_ge(side_ready, n + 1)
                act.activation(qaT[:, h, :], side[:, n % 4], ACT.Copy).then_inc(side_read[n % 4], 2)

            for g in range(NG):
                nxt = KT * (g + 1)
                for j in range(KT - 1):
                    if nxt + j < C_OUT:
                        split_hi(nxt + j)
                    if g == G_IDX and j == 2:
                        act.wait_ge(trig_arg_ready, 1)
                        act.activation(trig[:, :, :, :].rearrange("p a t f -> p (a t f)"), trig_tmp[:, 0, :],
                                       ACT.Sin).then_inc(trig_ready, 1)
                    if g == G_Q:
                        if j == 0:
                            for n in range(4):
                                evac_idxT(n)
                        elif j == 1:
                            for n in range(4, F_LOGIT):
                                evac_idxT(n)
                        else:
                            for i in range(4 * (j - 2), 4 * (j - 1)):
                                relu_unit(i)
                    if g == G_GA and j >= QT_AT:
                        evac_qT(2 * (j - QT_AT))
                        evac_qT(2 * (j - QT_AT) + 1)
                evac_group(g)
                if g == G_Q:
                    for i in range(4 * (KT - 3), 4 * (KT - 2)):
                        relu_unit(i)
                if g == G_V:
                    evac_lat_hi()
                if g == G_GA:
                    for h in range(2 * (KT - 1 - QT_AT), A_HEADS):
                        evac_qT(h)
                if nxt + KT - 1 < C_OUT:
                    split_hi(nxt + KT - 1)

            for m in range(TT):
                act.wait_ge(acc_ready, A_QPE + m + 1)
                act.activation(qpe_tok[:, m, :], acc[:, m, 0:B_HEADS * ROPE_D], ACT.Copy).then_inc(acc_read[m], 2)
            for first, dst in ((A_QN, qbT), (A_KN, kbT)):
                for p in range(4):
                    act.wait_ge(acc_ready, first + p + 1)
                    act.activation(dst[0:NOPE, 2 * p, :], acc[0:NOPE, p], ACT.Copy).then_inc(acc_read[p], 1)
            for m in range(TT):
                act.wait_ge(acc_ready, A_VB + m + 1)
                act.activation(vb[:, m, :], acc[:, m], ACT.Copy).then_inc(acc_read[m], 2)

            def evac_qpeT(j):
                quad, r = divmod(j, 2)
                act.wait_ge(acc_ready, A_END + quad + 1)
                ins = act.activation(qbT[NOPE:B_QK, 4 * quad + r, :], ps_y[32 * r:32 * r + 32, quad], ACT.Copy)
                if r == 1:
                    ins.then_inc(acc_read[2 + quad], 1)

            def exp_unit(u):
                N = unit(u)[3]
                act.wait_ge(masked_ready, u + 1)
                act.activation(probs[:, u % NPROBS, 0:N], probs[:, u % NPROBS, 0:N], ACT.Exp, bias=neg_max[:, u % 8:u % 8 + 1],
                               scale=-1.0, accum_out=row_sum[:, u:u + 1]).then_inc(probs_ready, 1)

            def copy_probsT(u):
                N = unit(u)[3]
                act.wait_ge(transposed, slot_of[u] + 1)
                if u >= 3:
                    act.wait_ge(pv_done, u - 2)
                act.activation(probsT[:, u % 3, 0:N], ps_pT[:, slot_of[u] % 2, 0:N], ACT.Copy).then_inc(probsT_copied, 1)

            def copy_oT_hi(i, b):
                n = slot_of[i, b]
                if i >= 2 and b == 0:
                    act.wait_ge(out_ps_ready, 2 * (i - 1))
                act.wait_ge(transposed, n + 1)
                act.activation((oT0, oT1)[i % 2][:, 0, 4 * b:4 * b + 4, :],
                               ps_pT[:, n % 2].rearrange("p (a b) -> p a b", a=4), ACT.Copy).then_inc(oT_hi_ready, 1)

            for u in range(NU + T_LAG):
                if u >= T_LAG:
                    copy_probsT(u - T_LAG)
                i, j = divmod(u - NU_A, HEADS)
                if 0 < i < TT and OT_AT <= j < OT_AT + 2:
                    copy_oT_hi(i - 1, j - OT_AT)
                if u < NU:
                    exp_unit(u)
                if 0 <= u - PET_AT - 1 < 4:
                    evac_qpeT(u - PET_AT - 1)
                if u == PET_AT + 7:
                    act.wait_ge(acc_ready, A_END + 3)
                    act.activation(kbT[NOPE:B_QK, 0, :], ps_y[0:ROPE_D, 0], ACT.Copy).then_inc(acc_read[2], 2)
                if 0 <= u - WO_LATE < RING:
                    split_hi(C_OUT + RING + u - WO_LATE)
            for b in range(2):
                copy_oT_hi(TT - 1, b)

        @block.vector
        def _(dve):
            count = [0]

            def step(ins):
                ins.then_inc(dve_step, 1)
                count[0] += 1
                return count[0]

            def after(ins):
                dve.wait_ge(dve_step, step(ins))

            V = nc.vector

            def x_low(k):
                dve.wait_ge(x_loaded[k if k < 2 else 1 + k // 2], 16)
                dve.wait_ge(x_hi_ready, k + 1)
                V.tensor_tensor(x_lo[:, k, :], x_raw[:, k, :], x_hi[:, k, :], ALU.subtract).then_inc(x_lo_ready, 1)

            for k in range(4):
                x_low(k)

            nt = TT * NFREQ
            ang, turns = trig_tmp[:, 0, :], trig_tmp[:, 1, :]
            ROUND = 1.5 * 2 ** 23
            two_pi = 2 * np.pi
            C1 = 6.28125
            C2 = float(np.round((two_pi - C1) * 2 ** 20) / 2 ** 20)
            C3 = float(two_pi - C1 - C2)
            dve.wait_ge(pos_loaded, 32)
            after(V.tensor_copy(pos_f, pos_i[:, :]))
            for half in range(2):
                dst = ang[:, half * nt:(half + 1) * nt].rearrange("p (t f) -> p t f", t=TT)
                last = step(V.tensor_tensor(dst, pos_f.unsqueeze(2).broadcast_to([P, TT, NFREQ]),
                                            freq_sb[:, :].unsqueeze(1).broadcast_to([P, TT, NFREQ]), ALU.mult))
            dve.wait_ge(dve_step, last)
            for half in range(2):
                s = slice(half * nt, (half + 1) * nt)
                last = step(V.tensor_scalar(turns[:, s], ang[:, s], float(1 / two_pi), 0.25 * half, ALU.mult, ALU.add))
            dve.wait_ge(dve_step, last)
            after(V.tensor_scalar(turns, turns, ROUND, ROUND, ALU.add, ALU.subtract))
            for c in (C1, C2, C3):
                after(V.scalar_tensor_tensor(out=ang, in0=turns, scalar=-c, in1=ang, op0=ALU.mult, op1=ALU.add))
            after(V.tensor_scalar(ang[:, nt:], ang[:, nt:], float(np.pi / 2), None, ALU.add))
            V.tensor_scalar(ang, ang, 3.1415925, -3.1415925, ALU.min, ALU.max).then_inc(trig_arg_ready, 1)
            for k in range(4, KT):
                x_low(k)

            def rope(dst, src, m, heads, half, f0, wait=None):
                n = heads * 2 * half
                s4 = src.rearrange("p (h a f) -> p h a f", a=2, f=half)
                d4 = dst.rearrange("p (h a f) -> p h a f", a=2, f=half)
                t1 = tmp[:, 0, 0:n].rearrange("p (h a f) -> p h a f", a=2, f=half)
                t2 = tmp[:, 1, 0:n].rearrange("p (h a f) -> p h a f", a=2, f=half)
                cos = trig[:, 1, m, f0:f0 + half].unsqueeze(1).broadcast_to([P, heads, half])
                sin = trig[:, 0, m, f0:f0 + half].unsqueeze(1).broadcast_to([P, heads, half])
                for a in range(2):
                    step(V.tensor_tensor(t1[:, :, a], s4[:, :, a], cos, ALU.mult))
                    last = step(V.tensor_tensor(t2[:, :, a], s4[:, :, 1 - a], sin, ALU.mult))
                dve.wait_ge(dve_step, last)
                step(V.tensor_tensor(d4[:, :, 0], t1[:, :, 0], t2[:, :, 0], ALU.subtract))
                after(V.tensor_tensor(d4[:, :, 1], t1[:, :, 1], t2[:, :, 1], ALU.add))

            nrot = (IDX_HEADS + 1) * IDX_DIM
            dve.wait_ge(trig_ready, 1)
            for m in range(TT):
                wait_tok(dve, G_IDX, m)
            for k in range(2):
                dve.wait_ge((x_hi_ready, x_lo_ready)[k], KT)
            step(V.tensor_scalar(iw.rearrange("p (t h) -> p t h", t=TT), idx_tok[:, :, nrot:N_IDX],
                                 IDX_HEADS ** -0.5, None, ALU.mult))
            for m in range(TT):
                rope(idx_tok[:, m, 0:nrot], idx_tok[:, m, 0:nrot], m, IDX_HEADS + 1, FREQ_B, FREQ_A)
                q3 = idx_tok[:, m, 0:IDX_HEADS * IDX_DIM].rearrange("p (h d) -> p h d", d=IDX_DIM)
                k2 = idx_tok[:, m, IDX_HEADS * IDX_DIM:nrot]
                k3 = k2.unsqueeze(1).broadcast_to([P, 2, IDX_DIM])
                if m > 0:
                    st = iq_st[:, m - 1]
                    for a in (0, 2):
                        last = step(V.tensor_copy(st[:, :, a].bitcast(f32r), q3))
                kst = ik_st[:, m]
                last = step(V.tensor_copy(kst[:, 0:2].bitcast(f32r), k3))
                dve.wait_ge(dve_step, last)
                if m > 0:
                    for a in (1, 3):
                        last = step(V.tensor_tensor(st[:, :, a].bitcast(f32r), q3, st[:, :, 0], ALU.subtract))
                V.tensor_tensor(kst[:, 2:4].bitcast(f32r), k3, kst[:, 0:2], ALU.subtract).then_inc(idx_split, 1)

            dve.wait_ge(idx_split, TT)
            for m in range(TT):
                wait_tok(dve, G_LAT, m)
                for j, (a, b) in enumerate(((0, Q_LORA), (Q_LORA, Q_LORA + KV_LORA))):
                    src = lat_tok[:, m, a:b]
                    last = step(V.tensor_tensor_reduce(out=tmp[:, m % 2, a:b], in0=src, in1=src, scale=1.0, scalar=0.0,
                                                       op0=ALU.mult, op1=ALU.add, accum_out=ssq[:, 2 * m + j:2 * m + j + 1]))
                dve.wait_ge(dve_step, last)
            ssq2, lat_r2 = (v.rearrange("p (t j) -> p t j", j=2) for v in (ssq, lat_r))
            for j, n in enumerate((Q_LORA, KV_LORA)):
                last = step(V.tensor_scalar(lat_r2[:, :, j], ssq2[:, :, j], 1.0 / n, RMS_EPS, ALU.mult, ALU.add))
            dve.wait_ge(dve_step, last)
            dve.sem_inc(lat_ms_ready, 1)
            dve.wait_ge(lat_rs_ready, 1)
            for m in range(TT):
                for j, (a, b) in enumerate(((0, Q_LORA), (Q_LORA, Q_LORA + KV_LORA))):
                    last = V.tensor_scalar(lat_tok[:, m, a:b], lat_tok[:, m, a:b], lat_r[:, 2 * m + j:2 * m + j + 1],
                                           None, ALU.mult).then_inc(lat_normed, 1)
            for m in range(TT):
                rope(kpe_tok[:, m, :], lat_tok[:, m, Q_LORA + KV_LORA:N_LAT], m, 1, FREQ_B, FREQ_A)
                dve.sem_inc(kpe_rotated, 1)

            dve.wait_ge(const_ready, 5)
            for i in range((TT - 1) * IDX_HEADS):
                m, h = 1 + i // IDX_HEADS, i % IDX_HEADS
                N = (m + 1) * P
                sc = score[:, SCORE_AT[m]:SCORE_AT[m] + N]
                n = F_LOGIT + i
                dve.wait_ge(side_read[n % 4], seen(n) + 2)
                if h > 0:
                    dve.wait_ge(relu_used, i)
                V.scalar_tensor_tensor(out=sc, in0=relu[:, i % 4, 0:N], scalar=iw[:, m * IDX_HEADS + h:m * IDX_HEADS + h + 1],
                                       in1=causal[:, SEQ - N:SEQ] if h == 0 else sc, op0=ALU.mult,
                                       op1=ALU.add).then_inc(relu_used, 1)
            dve.wait_ge(relu_used, (TT - 1) * IDX_HEADS)

            spans = [score[:, SCORE_AT[m]:SCORE_AT[m] + (m + 1) * P] for m in range(1, TT)]
            for r in range(TOP_K // 8):
                for j, sc in enumerate(spans):
                    if r > 0:
                        dve.wait_ge(dve_step, count[0] - 2)
                    step(V.max(top8[:, 8 * j:8 * j + 8], sc))
                for j, sc in enumerate(spans):
                    dve.wait_ge(dve_step, count[0] - 2)
                    step(V.match_replace(out=sc, in_to_replace=top8[:, 8 * j:8 * j + 8], in_values=sc, imm_value=TAKEN))
            dve.wait_ge(dve_step, count[0])
            V.tensor_scalar(score[:, :], score[:, :], TAKEN, NEG, ALU.not_equal, ALU.mult).then_inc(bias_ready, 1)

            for t in range(QL_T + 1):
                n = F_LAT + t
                dve.wait_ge(lat_hi_ready, t + 1)
                V.scalar_tensor_tensor(out=latT_lo[:, t, :], in0=side[:, n % 4], scalar=gq[:, t:t + 1] if t < QL_T else gkv,
                                       in1=latT_hi[:, t, :], op0=ALU.mult, op1=ALU.subtract).then_inc(side_read[n % 4], 2)

            def split_parts(dst, src, done):
                d, v = dst, src.rearrange("p (h d) -> p h d", d=A_DIM)
                after(V.tensor_copy(d[:, :, 0].bitcast(f32r), v))
                V.tensor_tensor(d[:, :, 1].bitcast(f32r), v, d[:, :, 0], ALU.subtract).then_inc(done, 1)

            dve.wait_ge(side_ready, F_LOGIT)
            for m in range(TT):
                dve.wait_ge(q_rotated, 2 * (m + 1))
                split_parts(q_st[:, m], q_tok[:, m, :], q_split)
            for m in range(TT):
                wait_tok(dve, G_K, m)
                rope(k_tok[:, m, :], k_tok[:, m, :], m, A_HEADS, FREQ_A, 0)
                split_parts(k_st[:, m], k_tok[:, m, :], k_split)

            for h in range(A_HEADS):
                n = F_KT + h
                dve.wait_ge(side_ready, n + 1)
                V.tensor_copy(kaT[:, h, :], side[:, n % 4]).then_inc(side_read[n % 4], 2)
            for first, dst in ((A_QN, qbT), (A_KN, kbT)):
                for p in range(4):
                    dve.wait_ge(acc_ready, first + p + 1)
                    V.tensor_copy(dst[0:NOPE, 2 * p + 1, :], acc[NOPE:P, p]).then_inc(acc_read[p], 1)

            def evac_qpeT(j):
                quad, r = divmod(j, 2)
                dve.wait_ge(acc_ready, A_END + quad + 1)
                ins = V.tensor_copy(qbT[NOPE:B_QK, 4 * quad + 2 + r, :], ps_y[64 + 32 * r:96 + 32 * r, quad])
                if r == 1:
                    ins.then_inc(acc_read[2 + quad], 1)

            def mask_unit(u):
                v, m, h, N = unit(u)
                a = v < TT
                bias = spans[m - 1] if a and m > 0 else causal[:, SEQ - N:SEQ]
                scale = (A_DIM if a else B_QK) ** -0.5
                dve.wait_ge(scores_ready, u + 1)
                if u == 0:
                    dve.wait_ge(bias_ready, 1)
                if u >= NPROBS:
                    dve.wait_ge(transposed, slot_of[u - NPROBS] + 1)
                V.tensor_tensor_reduce(out=probs[:, u % NPROBS, 0:N], in0=ps_s[:, u % 2, 0:N], in1=bias, scale=-scale,
                                       scalar=3.0e38, op0=ALU.add, op1=ALU.min,
                                       accum_out=neg_max[:, u % 8:u % 8 + 1]).then_inc(masked_ready, 1)

            def normalise(v):
                m = ORDER[v % TT]
                cols = slice(A_WIDTH * (v // TT), A_WIDTH * (v // TT + 1))
                dve.wait_ge(pv_done, HEADS * (v + 1))
                after(V.reciprocal(rinv, row_sum[:, HEADS * v:HEADS * (v + 1)]))
                V.tensor_tensor(o_norm[:, :].rearrange("p (h d) -> p h d", h=HEADS),
                                ps_o[:, v % 2].rearrange("p (h d) -> p h d", h=HEADS),
                                rinv.unsqueeze(2).broadcast_to([P, HEADS, A_DIM]), ALU.mult).then_inc(o_ps_read, 1)
                dve.wait_ge(o_ps_read, v + 1)
                wait_tok(dve, G_GB if v >= TT else G_GA, m)
                V.tensor_tensor(gate[:, m, cols], o_norm[:, :], gate[:, m, cols], ALU.mult).then_inc(o_ready, 1)

            def copy_oT_lo(i, b):
                dst = (oT0, oT1)[i % 2]
                dve.wait_ge(oT_hi_ready, 2 * i + b + 1)
                V.tensor_tensor(dst[:, 1, 4 * b:4 * b + 4, :], ps_pT[:, slot_of[i, b] % 2].rearrange("p (a b) -> p a b", a=4),
                                dst[:, 0, 4 * b:4 * b + 4, :], ALU.subtract).then_inc(oT_lo_ready, 1)

            def wo_high(j):
                c = C_OUT + j
                dve.wait_ge(w_loaded[(c // 2) % RPAIR], 16 * (c // 2 // RPAIR + 1))
                if j == 0:
                    dve.wait_ge(acc_ready, A_END)
                V.tensor_copy(wo_hi[:, j // 2, j % 2], w_raw[:, c % RING, :]).then_inc(wo_hi_ready, 1)

            def wo_low(k):
                c = C_OUT + 2 * k + 1
                dve.wait_ge(w_loaded[(c // 2) % RPAIR], 16 * (c // 2 // RPAIR + 1))
                wait_wo_hi(dve, c - C_OUT)
                if k == 0:
                    dve.wait_ge(scores_ready, NU_A)
                V.tensor_tensor(wo_lo(k, 1), w_raw[:, c % RING, :], wo_hi[:, k, 1], ALU.subtract).then_inc(wo_lo_ready, 1)

            def ln_residual(i, b):
                src = ps_s if i == TT - 1 else ps_y
                cols = slice(BANK * b, BANK * (b + 1))
                if b == 0:
                    dve.wait_ge(xres_loaded[i % 2], 16 * (i // 2 + 1))
                    if i > 0:
                        dve.wait_ge(stored, 32 * i)
                dve.wait_ge(out_ps_ready, 2 * i + b + 1)
                V.scalar_tensor_tensor(out=y[:, cols], in0=x_res[:, i % 2, cols], scalar=ALPHA, in1=src[:, b],
                                       op0=ALU.mult, op1=ALU.add).then_inc(out_ps_read, 1)
                dve.wait_ge(out_ps_read, 2 * i + b + 1)
                step(V.bn_stats(stats[:, 6 * b:6 * b + 6], y[:, cols]))

            def ln_stats(i):
                dve.wait_ge(dve_step, count[0])
                after(V.bn_aggr(aggr[:, 0:2], stats))
                V.tensor_scalar(aggr[:, 2:3], aggr[:, 1:2], LN_EPS, None, ALU.add).then_inc(var_ready, 1)

            def ln_centre(i, b):
                cols = slice(BANK * b, BANK * (b + 1))
                if i == 0 and b == 0:
                    dve.wait_ge(ln_loaded, 32)
                step(V.scalar_tensor_tensor(out=y[:, cols], in0=y[:, cols], scalar=aggr[:, 0:1], in1=lng[:, cols],
                                            op0=ALU.subtract, op1=ALU.mult))

            def ln_scale(i, b):
                cols = slice(BANK * b, BANK * (b + 1))
                dve.wait_ge(dve_step, count[0])
                dve.wait_ge(rstd_ready, i + 1)
                V.scalar_tensor_tensor(out=y[:, cols], in0=y[:, cols], scalar=rstd, in1=lnb[:, cols],
                                       op0=ALU.mult, op1=ALU.add).then_inc(y_ready, 1)

            def ln_schedule(t):
                u = OUT_AT[t]
                return [(u + 5, lambda: ln_residual(t, 0)), (u + 8, lambda: ln_residual(t, 1)), (u + 9, lambda: ln_stats(t)),
                        (u + 9, lambda: ln_centre(t, 0)), (u + 10, lambda: ln_centre(t, 1)),
                        (u + 10, lambda: ln_scale(t, 0)), (u + 11, lambda: ln_scale(t, 1))]

            for u in range(NU):
                mask_unit(u)
                v, j = divmod(u, HEADS)
                i = v - TT
                if v > 0 and j == PV_LAG:
                    normalise(v - 1)
                if 0 < u <= TT:
                    wait_tok(dve, A_QPE // TT, u - 1)
                    rope(qpe_tok[:, u - 1, :], qpe_tok[:, u - 1, :], u - 1, B_HEADS, FREQ_B, FREQ_A)
                    dve.sem_inc(qpe_rotated, 1)
                if 0 <= u - PET_AT - 1 < 4:
                    evac_qpeT(u - PET_AT - 1)
                if 0 <= u - WO_EARLY < RING:
                    wo_high(u - WO_EARLY)
                if 0 <= u - NU_A < 4:
                    wo_low(u - NU_A)
                if 0 <= u - WO_LATE - 1 < RING and (u - WO_LATE - 1) % 2 == 0:
                    wo_low(4 + (u - WO_LATE - 1) // 2)
                if 0 < i and OT_AT <= j < OT_AT + 2:
                    copy_oT_lo(i - 1, j - OT_AT)
                for t in range(TT - 2):
                    for at_u, take in ln_schedule(t):
                        if at_u == u:
                            take()
            normalise(NPASS - 1)
            for b in range(2):
                copy_oT_lo(TT - 1, b)
            for t in range(TT):
                for at_u, take in ln_schedule(t):
                    if at_u >= NU or t >= TT - 2:
                        take()

        @block.tensor
        def _(pe):
            mm = nc.tensor.matmul

            def products(dst, pairs, start, stop):
                for j, (a, b) in enumerate(pairs):
                    ins = mm(dst, a, b, start=start and j == 0, stop=stop and j == len(pairs) - 1)
                return ins

            def group(g, beside=None):
                n = GROUPS[g][1]
                for k in range(KT):
                    c = KT * g + k
                    s = c % RING
                    if c == 0:
                        pe.wait_ge(x_hi_ready, 1)
                        pe.wait_ge(w_hi_ready, 1)
                        for j, (xp, wp) in enumerate(((x_hi, w_hi), (x_lo, w_hi), (x_hi, w_lo))):
                            if j > 0:
                                pe.wait_ge((x_lo_ready, w_lo_ready)[j - 1], 1)
                            for m in range(TT):
                                ins = mm(acc[:, m, 0:n], xp[:, 0, m * P:(m + 1) * P], wp[:, 0, 0:n], start=j == 0, stop=False)
                        ins.then_inc(chunk_used, 1)
                        continue
                    if g == 0:
                        pe.wait_ge(x_hi_ready, k + 1)
                        pe.wait_ge(x_lo_ready, k + 1)
                    pe.wait_ge(w_hi_ready, c + 1)
                    pe.wait_ge(w_lo_ready, c + 1)
                    for m in range(TT):
                        if k == 0 and g > 0:
                            pe.wait_ge(acc_read[m], 2 * g)
                        t = slice(m * P, (m + 1) * P)
                        wh, wl = w_hi[:, s, 0:n], w_lo[:, s, 0:n]
                        ins = products(acc[:, m, 0:n], ((x_hi[:, k, t], wh), (x_hi[:, k, t], wl), (x_lo[:, k, t], wh)),
                                       k == 0, k == KT - 1)
                        if k == KT - 1:
                            ins.then_inc(acc_ready, 1)
                        elif m == TT - 1:
                            ins.then_inc(chunk_used, 1)
                    if beside:
                        beside(g, k)

            def fill(n):
                if n >= 4:
                    pe.wait_ge(side_read[n % 4], seen(n))
                return side[:, n % 4]

            def idx_transposes(n):
                if n == 0:
                    pe.wait_ge(idx_split, TT)
                    pe.wait_ge(const_ready, 5)
                bank = fill(n)
                for j in range(4):
                    if n < F_IK:
                        m, quad = divmod(n, 2)
                        src = iq_st[:, m, 4 * quad + j].rearrange("p a d -> p (a d)")
                    else:
                        src = ik_st[:, j].rearrange("p a d -> p (a d)")
                    ins = nc.tensor.transpose(bank[:, j * P:(j + 1) * P], src, ident[:, :])
                ins.then_inc(side_ready, 1)

            def idx_logits(i):
                m, h = 1 + i // IDX_HEADS, i % IDX_HEADS
                N = (m + 1) * P
                bank = fill(F_LOGIT + i)
                if i == 0:
                    for n in range(F_IK - 3, F_IK + 1):
                        pe.wait_ge(side_read[n % 4], seen(n) + 2)
                mm(bank[:, 0:N], iqT[:, h, (m - 1) * P:m * P], ikT[:, 0:N], start=True, stop=True).then_inc(side_ready, 1)

            def lat_transposes():
                pe.wait_ge(lat_normed, 2 * TT)
                for t in range(QL_T + 1):
                    bank = fill(F_LAT + t)
                    for m in range(TT):
                        ins = nc.tensor.transpose(bank[:, m * P:(m + 1) * P], lat_tok[:, m, t * P:(t + 1) * P], ident[:, :])
                    ins.then_inc(side_ready, 1)

            def a_transposes(first, src, h):
                bank = fill(first + h)
                for m in range(TT):
                    if h == 0:
                        pe.wait_ge(q_split if first == F_QT else k_split, m + 1)
                    ins = nc.tensor.transpose(bank[:, m * P:(m + 1) * P], src[:, m, h].rearrange("p a d -> p (a d)"), ident[:, :])
                ins.then_inc(side_ready, 1)

            def beside(g, k):
                if g == G_Q:
                    if k < 2:
                        for n in range(4 * k, min(4 * k + 4, F_LOGIT)):
                            idx_transposes(n)
                    else:
                        for i in range(4 * (k - 2), 4 * (k - 1)):
                            idx_logits(i)
                if g == G_V and k == KT - 1:
                    lat_transposes()
                if g == G_GA and k >= QT_AT:
                    a_transposes(F_QT, q_st, 2 * (k - QT_AT))
                    a_transposes(F_QT, q_st, 2 * (k - QT_AT) + 1)
                if g == G_GA and k == KT - 1:
                    for h in range(2 * (KT - QT_AT), A_HEADS):
                        a_transposes(F_QT, q_st, h)
                if g == G_GB and k >= KT_AT:
                    a_transposes(F_KT, k_st, 2 * (k - KT_AT))
                    a_transposes(F_KT, k_st, 2 * (k - KT_AT) + 1)

            pe.wait_ge(warm_ready, 1)
            for _ in range(NWARM):
                mm(side[:, 0, 0:P], warm[:, :], warm[:, :], start=True, stop=True)
            for g in range(NG):
                group(g, beside)

            def wait_chunk(c):
                pe.wait_ge(w_hi_ready, c + 1)
                pe.wait_ge(w_lo_ready, c + 1)

            for n in range(F_LAT, F_LAT + QL_T + 1):
                pe.wait_ge(side_read[n % 4], seen(n) + 2)
            npe = B_HEADS * ROPE_D
            wait_chunk(C_UQP + 1)
            for m in range(TT):
                pe.wait_ge(acc_read[m], seen(A_QPE + m))
                t0 = slice(m * P, (m + 1) * P)
                for t in range(QL_T):
                    s = (C_UQP + t) % RING
                    ins = products(acc[:, m, 0:npe], ((latT_hi[:, t, t0], w_hi[:, s, 0:npe]), (latT_hi[:, t, t0], w_lo[:, s, 0:npe]),
                                                      (latT_lo[:, t, t0], w_hi[:, s, 0:npe])), t == 0, t == QL_T - 1)
                ins.then_inc(acc_ready, 1)
            for p in range(4):
                pe.wait_ge(acc_read[p], seen(A_QN + p))
                for t in range(QL_T):
                    s, cols = (C_UQN + t) % RING, slice(p * P, (p + 1) * P)
                    ins = products(acc[:, p], ((w_hi[:, s, cols], latT_hi[:, t, :]), (w_hi[:, s, cols], latT_lo[:, t, :]),
                                               (w_lo[:, s, cols], latT_hi[:, t, :])), t == 0, t == QL_T - 1)
                ins.then_inc(acc_ready, 1)
            wait_chunk(C_UKV)
            for p in range(4):
                pe.wait_ge(acc_read[p], seen(A_KN + p))
                s, cols = C_UKN % RING, slice(p * P, (p + 1) * P)
                products(acc[:, p], ((w_hi[:, s, cols], latT_hi[:, QL_T, :]), (w_hi[:, s, cols], latT_lo[:, QL_T, :]),
                                     (w_lo[:, s, cols], latT_hi[:, QL_T, :])), True, True).then_inc(acc_ready, 1)
            for m in range(TT):
                pe.wait_ge(acc_read[m], seen(A_VB + m))
                s, t0 = C_UKV % RING, slice(m * P, (m + 1) * P)
                products(acc[:, m], ((latT_hi[:, QL_T, t0], w_hi[:, s, :]), (latT_hi[:, QL_T, t0], w_lo[:, s, :]),
                                     (latT_lo[:, QL_T, t0], w_hi[:, s, :])), True, True).then_inc(acc_ready, 1)

            def qpe_transposes():
                pe.wait_ge(qpe_rotated, TT)
                for quad in range(2):
                    pe.wait_ge(acc_read[2 + quad], seen(A_QPET + quad))
                    for m in range(TT):
                        ins = nc.tensor.transpose(ps_y[:, quad, m * P:(m + 1) * P], qpe_tok[:, m, quad * P:(quad + 1) * P], ident[:, :])
                    ins.then_inc(acc_ready, 1)

            def kpe_transposes():
                pe.wait_ge(kpe_rotated, TT)
                pe.wait_ge(acc_read[2], seen(A_KPET))
                for m in range(TT):
                    ins = nc.tensor.transpose(ps_y[0:ROPE_D, 0, m * P:(m + 1) * P], kpe_tok[:, m, :], ident[:, :])
                ins.then_inc(acc_ready, 1)

            def scores(u):
                v, m, h, N = unit(u)
                b = u % 2
                if u < 2:
                    pe.wait_ge(side_read[b], SIDE_LAST[b])
                else:
                    pe.wait_ge(masked_ready, u - 1)
                t = slice(m * P, (m + 1) * P)
                if v < TT:
                    if u == 0:
                        for n in range(F_KT - 4, F_KT + A_HEADS):
                            pe.wait_ge(side_read[n % 4], seen(n) + 2)
                    mm(ps_s[:, b, 0:N], qaT[:, h, t], kaT[:, h, 0:N], start=True, stop=False)
                    if u == 0:
                        pe.wait_ge(kaT_swapped, 32)
                    ins = mm(ps_s[:, b, 0:N], qaT[:, h, t], kaT_swap[:, h, 0:N], start=False, stop=True)
                else:
                    if u == NU_A:
                        for p in range(4):
                            pe.wait_ge(acc_read[p], ACC_LAST[p])
                        pe.wait_ge(kpe_copied, 16)
                    ins = mm(ps_s[:, b, 0:N], qbT[:, h, t], kbT[:, h, 0:N], start=True, stop=True)
                ins.then_inc(scores_ready, 1)

            def slot(n):
                if n < 2:
                    pe.wait_ge(side_read[2 + n], SIDE_LAST[2 + n])
                elif isinstance(slots[n - 2], int):
                    pe.wait_ge(probsT_copied, slots[n - 2] + 1)
                else:
                    i, b = slots[n - 2]
                    pe.wait_ge(oT_lo_ready, 2 * i + b + 1)
                return ps_pT[:, n % 2]

            def transposes(u):
                v, m, h, N = unit(u)
                bank = slot(slot_of[u])
                pe.wait_ge(probs_ready, u + 1)
                for j in range(m + 1):
                    ins = nc.tensor.transpose(bank[:, j * P:(j + 1) * P], probs[:, u % NPROBS, j * P:(j + 1) * P], ident[:, :])
                ins.then_inc(transposed, 1)

            def outputs(u):
                v, m, h, N = unit(u)
                if h == 0:
                    if v < 2:
                        pe.wait_ge(acc_read[v], ACC_LAST[v])
                    else:
                        pe.wait_ge(o_ps_read, v - 1)
                    if v == 0:
                        for t in range(TT):
                            wait_tok(pe, G_V, t)
                pe.wait_ge(probsT_copied, u + 1)
                vals = va if v < TT else vb
                for j in range(m + 1):
                    ins = mm(ps_o[:, v % 2, h * A_DIM:(h + 1) * A_DIM], probsT[:, u % 3, j * P:(j + 1) * P],
                             vals[:, j, h * A_DIM:(h + 1) * A_DIM], start=(j == 0), stop=(j == m))
                ins.then_inc(pv_done, 1)

            def o_transposes(i, b):
                m = ORDER[i]
                bank = slot(slot_of[i, b])
                pe.wait_ge(o_ready, TT + i + 1)
                for j in range(4):
                    ins = nc.tensor.transpose(bank[:, j * P:(j + 1) * P], gate[:, m, (4 * b + j) * P:(4 * b + j + 1) * P], ident[:, :])
                ins.then_inc(transposed, 1)

            def out_products(i, a, z):
                last = i == TT - 1
                for n in range(a, z):
                    b, r = divmod(n, 3 * KT)
                    k, j = divmod(r, 3)
                    if n == 0:
                        pe.wait_ge(oT_hi_ready, 2 * i + 2)
                        pe.wait_ge(oT_lo_ready, 2 * i + 2)
                        if i == 0:
                            pe.wait_ge(w_lo_ready, C_OUT + KT)
                            pe.wait_ge(wo_lo_ready, KT)
                    if r == 0:
                        if last:
                            pe.wait_ge(masked_ready, NU)
                        elif i == 0:
                            pe.wait_ge(acc_read[2 + b], ACC_LAST[2 + b])
                        else:
                            pe.wait_ge(out_ps_read, 2 * i - 1 + b)
                    o, w = ((0, wo_hi[:, k, b]), (0, wo_lo(k, b)), (1, wo_hi[:, k, b]))[j]
                    ins = mm((ps_s if last else ps_y)[:, b], oT[i % 2][:, o, k, :], w, start=(r == 0), stop=(r == 3 * KT - 1))
                    if r == 3 * KT - 1:
                        ins.then_inc(out_ps_ready, 1)

            oT = (oT0, oT1)
            NSTEP = 6 * KT
            per = NSTEP // HEADS
            for u in range(NU + PV_LAG):
                if u < NU:
                    scores(u)
                if 0 <= u - T_LAG < NU:
                    transposes(u - T_LAG)
                if u - PV_LAG >= 0:
                    outputs(u - PV_LAG)
                if u == PET_AT:
                    qpe_transposes()
                if u == PET_AT + 6:
                    kpe_transposes()
                i, j = divmod(u - NU_A, HEADS)
                if 0 < i < TT and OT_AT <= j < OT_AT + 2:
                    o_transposes(i - 1, j - OT_AT)
                for t in range(TT - 1):
                    if 0 <= u - OUT_AT[t] < HEADS:
                        out_products(t, per * (u - OUT_AT[t]), per * (u - OUT_AT[t] + 1))
            done = per * (NU + PV_LAG - OUT_AT[TT - 2])
            out_products(TT - 2, done, NSTEP)
            for b in range(2):
                o_transposes(TT - 1, b)
            out_products(TT - 1, 0, NSTEP)


NWARM = 12
T_LAG, PV_LAG = 3, 4
NPROBS = 5
OT_AT = 5
QT_AT, KT_AT = 4, 4
PET_AT = 8
WO_EARLY, WO_LATE = 14, 36
Q_ROTATE_AT = [28, 33, 38, 43]


def kernel(**inputs):
    import concourse.bacc as bacc
    from concourse.bass_utils import run_bass_kernel_spmd

    nc = bacc.Bacc("TRN2", target_bir_lowering=False, num_devices=1)
    a = {n: np.asarray(v) for n, v in inputs.items()}
    uq = a["w_uq"][0].reshape(Q_LORA, B_HEADS, B_QK)
    ukv = a["w_ukv"][0].reshape(KV_LORA, B_HEADS, NOPE + V_DIM)

    def parts(w, n):
        return np.concatenate([w[:, :, :n].reshape(w.shape[0], -1), w[:, :, n:].reshape(w.shape[0], -1)], axis=1)

    freqs = np.concatenate([np.float32(10000.0) ** (-np.arange(0, d, 2, dtype=np.float32) / np.float32(d))
                            for d in (A_DIM, ROPE_D)]).astype(np.float32)
    arrays = {
        "x": a["x"][0],
        "xT": a["x"][0].T,
        "positions": a["positions"][0].reshape(TT, P).T,
        "freqs": np.tile(freqs, (P, 1)),
        "w_in": a["w_in"][0],
        "q_norm_g": a["q_norm_g"][0].reshape(QL_T, P).T,
        "w_uq": parts(uq, NOPE),
        "kv_norm_g": a["kv_norm_g"][0].reshape(1, P).T,
        "w_ukv": parts(ukv, NOPE),
        "w_out": a["w_out"][0],
        "ln_g": a["ln_g"],
        "ln_b": a["ln_b"],
    }
    arrays = {n: np.ascontiguousarray(v) for n, v in arrays.items()}
    aps = {n: nc.dram_tensor(f"in_{n}", v.shape, mybir.dt.from_np(v.dtype), kind="ExternalInput").ap()
           for n, v in arrays.items()}
    out = nc.dram_tensor("out_y", (SEQ, D_MODEL), mybir.dt.float32, kind="ExternalOutput").ap()
    build(nc, out=out, **aps)
    r = run_bass_kernel_spmd(nc, [{f"in_{n}": v for n, v in arrays.items()}], core_ids=[0])
    return r.results[0]["out_y"].reshape(1, SEQ, D_MODEL)
```

```python
import numpy as np
import concourse.bass as bass
from concourse import mybir
from contextlib import ExitStack

P = 128
SEQ, D_MODEL = 512, 1024
TT = SEQ // P
KT = D_MODEL // P
A_HEADS, A_DIM = 8, 64
A_WIDTH = A_HEADS * A_DIM
IDX_HEADS, IDX_DIM = 8, 32
TOP_K = min(256, SEQ // 4)
B_HEADS, NOPE, ROPE_D, V_DIM = 8, 64, 32, 64
B_QK = NOPE + ROPE_D
Q_LORA, KV_LORA = 256, 128
QL_T = Q_LORA // P
ALPHA = 2 ** 0.25
LN_EPS, RMS_EPS = 1e-5, 1e-6
BANK = 512
FREQ_A, FREQ_B = A_DIM // 2, ROPE_D // 2
NFREQ = FREQ_A + FREQ_B
NEG = -3.0e38
TAKEN = -3.3e38


def build(nc, x, xT, positions, freqs, w_in, q_norm_g, w_uq, kv_norm_g, w_ukv, w_out, ln_g, ln_b, out):
    f32, f32r, i32 = mybir.dt.float32, mybir.dt.float32r, mybir.dt.int32
    ACT, ALU = mybir.ActivationFunctionType, mybir.AluOpType

    c0 = 4 * A_WIDTH
    N_IDX = IDX_HEADS * IDX_DIM + IDX_DIM + IDX_HEADS
    N_LAT = Q_LORA + KV_LORA + ROPE_D
    GROUPS = [(c0, N_IDX), (c0 + N_IDX, N_LAT), (0, BANK), (A_WIDTH, BANK), (2 * A_WIDTH, BANK),
              (3 * A_WIDTH, BANK), (c0 + N_IDX + N_LAT, BANK)]
    G_IDX, G_LAT, G_Q, G_K, G_V, G_GA, G_GB = range(7)
    NG = len(GROUPS)

    w_in_v = w_in.rearrange("(k p) c -> p k c", p=P)
    w_uq_v = w_uq.rearrange("(k p) c -> p k c", p=P)
    w_ukv_v = w_ukv.rearrange("p (s c) -> p s c", s=2)
    w_out_v = w_out.rearrange("(k p) (s c) -> p k s c", p=P, s=2)
    LOADS = [(w_in_v[:, 2 * q:2 * q + 2, c:c + n], n) for c, n in GROUPS for q in range(KT // 2)]
    C_UQN = 2 * len(LOADS)
    LOADS.append((w_uq_v[:, :, 0:B_HEADS * NOPE], B_HEADS * NOPE))
    C_UQP = 2 * len(LOADS)
    LOADS.append((w_uq_v[:, :, B_HEADS * NOPE:B_HEADS * B_QK], B_HEADS * ROPE_D))
    C_UKN = 2 * len(LOADS)
    C_UKV = C_UKN + 1
    LOADS.append((w_ukv_v, BANK))
    C_OUT = 2 * len(LOADS)
    LOADS += [(w_out_v[:, k], BANK) for k in range(KT)]
    RING = 8
    RPAIR = RING // 2

    def width(c):
        return LOADS[c // 2][1]

    ORDER = [3, 2, 1, 0]
    HEADS = A_HEADS
    NU_A = TT * HEADS
    NU = 2 * NU_A
    NPASS = 2 * TT
    NPAIR = TT * B_HEADS // 2

    def unit(u):
        v, h = divmod(u, HEADS)
        m = ORDER[v % TT]
        return v, m, h, (m + 1) * P

    O_AFTER = [NU_A + HEADS * (i + 1) + OT_AT - T_LAG for i in range(TT - 1)] + [NU]
    slots = []
    for u in range(NU + 1):
        if u < NU:
            slots.append(u)
        for i in range(TT):
            for b in range(2):
                if u == O_AFTER[i] + b * (i < TT - 1):
                    slots.append((i, b))
    OUT_AT = [NU_A + HEADS * (i + 1) + OT_AT + 2 for i in range(TT)]
    PIECES = [[slice(0, BANK), slice(BANK, D_MODEL)]] * (TT - 1) + [[slice(0, BANK), slice(BANK, BANK + BANK // 2),
                                                                    slice(BANK + BANK // 2, D_MODEL)]]
    slot_of = {x: n for n, x in enumerate(slots)}

    VB_ORDER = [3, 0, 1, 2]

    PAIR_AT = {NU_A + 2 * g + 2 + PV_LAG: g for g in range(NPAIR) if NU_A + 2 * g + 2 + PV_LAG < NU}
    PAIRS_LATE = NPAIR - len(PAIR_AT)

    base = -(-nc.sbuf_base // 64) * 64

    def sb(name, kib, shape, dt=f32):
        return nc.alloc_sbuf_tensor_at(name, shape, dt, offset=base + int(kib * 1024))

    x_hi = sb("x_hi", 0, [P, KT, SEQ], f32r)
    x_lo = sb("x_lo", 16, [P, KT, SEQ], f32r)
    qbT = sb("qbT", 0, [B_QK, B_HEADS, SEQ])
    kaT_swap = sb("kaT_swap", 178, [P, A_HEADS, SEQ], f32r)
    wo_lo_a = sb("wo_lo_a", 178, [P, KT // 2, 2, BANK], f32r)
    w_hi = sb("w_hi", 32, [P, RING, BANK], f32r)
    w_lo = sb("w_lo", 48, [P, RING, BANK], f32r)
    wo_hi = sb("wo_hi", 32, [P, KT, 2, BANK], f32r)
    w_raw = sb("w_raw", 64, [P, RING, BANK])
    qpe_tok = sb("qpe_tok", 76, [P, TT, B_HEADS * ROPE_D])
    x_res = sb("x_res", 64, [P, 2, D_MODEL])
    lng = sb("lng", 72, [P, D_MODEL])
    lnb = sb("lnb", 76, [P, D_MODEL])
    iqT = sb("iqT", 80, [P, IDX_HEADS, SEQ - P], f32r)
    ikT = sb("ikT", 92, [P, SEQ], f32r)
    latT_hi = sb("latT_hi", 80, [P, QL_T + 1, SEQ], f32r)
    latT_lo = sb("latT_lo", 86, [P, QL_T + 1, SEQ], f32r)
    oT0 = sb("oT0", 80, [P, 2, KT, P], f32r)
    o_norm = sb("o_norm", 92, [P, A_WIDTH])
    obT = sb("obT", 92, [P, B_HEADS // 2, P])
    tmp = sb("tmp", 94, [P, 2, BANK])
    y = sb("y", 94, [P, D_MODEL])
    y_last = sb("y_last", 0, [P, D_MODEL])
    x_raw = sb("x_raw", 98, [P, KT, SEQ])
    iq_st = sb("iq_st", 98, [P, TT - 1, IDX_HEADS, 4, IDX_DIM])
    ik_st = sb("ik_st", 110, [P, TT, 4, IDX_DIM])
    kaT = sb("kaT", 98, [P, A_HEADS, SEQ], f32r)
    wo_lo_b = sb("wo_lo_b", 98, [P, KT // 2, 2, BANK], f32r)
    q_tok = sb("q_tok", 114, [P, TT, A_WIDTH])
    k_tok = sb("k_tok", 122, [P, TT, A_WIDTH])
    kbT = sb("kbT", 114, [B_QK, B_HEADS, SEQ])
    relu = sb("relu", 130, [P, 4, BANK])
    q_tmp = sb("q_tmp", 130, [P, 2, BANK])
    vb = sb("vb", 130, [P, TT, B_HEADS * V_DIM])
    idx_tok = sb("idx_tok", 138, [P, TT, N_IDX])
    lat_tok = sb("lat_tok", 143, [P, TT, N_LAT])
    gate = sb("gate", 138, [P, TT, D_MODEL])
    warm = sb("warm", 154, [P, P])
    va = sb("va", 154, [P, TT, A_WIDTH])
    qaT = sb("qaT", 162, [P, A_HEADS, SEQ], f32r)
    oT1 = sb("oT1", 24, [P, 2, KT, P], f32r)
    probsT_b = sb("probsT_b", 162, [P, 3, 2, BANK], f32r)
    vb_parts = [sb(f"vb_parts{j}", kib, [P, B_HEADS // 2, 4, V_DIM], f32r) for j, kib in enumerate((174, 196, 130, 88))]
    probs = sb("probs", 16, [P, NPROBS, BANK])
    trig_tmp = sb("trig_tmp", 178, [P, 2, 2 * TT * NFREQ])
    probsT = sb("probsT", 26, [P, 3, BANK])
    causal = sb("causal", 194, [P, SEQ])
    score = sb("score", 196, [P, (2 + 3 + 4) * P])
    half_sum = sb("half_sum", 200, [P, 2, 2, P])
    trig = sb("trig", 200.5, [P, 2, TT, NFREQ])
    ident = sb("ident", 202, [P, P])
    kpe_tok = sb("kpe_tok", 202.5, [P, TT, ROPE_D])
    small = sb("small", 203, [P, 256])
    pos_i = sb("pos_i", 204, [P, TT], i32)
    freq_sb = sb("freq_sb", 204.25, [P, NFREQ])
    crossed = sb("crossed", 204.5, [P, 2, P])

    def wo_lo(k, half):
        return (wo_lo_a if k < KT // 2 else wo_lo_b)[:, k % (KT // 2), half]

    def y_of(i):
        return y_last if i == TT - 1 else y

    SCORE_AT = {1: 0, 2: 2 * P, 3: 5 * P}
    at = 0

    def col(n):
        nonlocal at
        at += n
        return small[:, at - n:at]

    pos_f, iw = col(TT), col(TT * IDX_HEADS)
    ssq, lat_r = col(2 * TT), col(2 * TT)
    gq, gkv = col(QL_T), col(1)
    top8 = col(8 * (TT - 1))
    neg_max, row_sum, rinv = col(8), col(NU), col(HEADS)
    stats, aggr, rstd = col(24), col(3), col(1)
    minus_half, unused = col(2 * TT), col(1)

    with ExitStack() as ctx:
        ps = ctx.enter_context(nc.psum_tensor("ps", [P, 8, BANK], f32))
        acc, side = ps[:, 0:4], ps[:, 4:8]
        ps_o, ps_y, ps_s, ps_pT = ps[:, 0:2], ps[:, 2:4], ps[:, 4:6], ps[:, 6:8]

        def sem(name):
            return ctx.enter_context(nc.semaphore(name))

        x_loaded = [sem(f"x_loaded{i}") for i in range(5)]
        w_loaded = [sem(f"w_loaded{i}") for i in range(RPAIR)]
        pos_loaded, norm_g_loaded, ln_loaded = sem("pos_loaded"), sem("norm_g_loaded"), sem("ln_loaded")
        xres_loaded = [sem(f"xres_loaded{i}") for i in range(2)]
        kaT_swapped, kpe_copied, stored = sem("kaT_swapped"), sem("kpe_copied"), sem("stored")
        const_ready = sem("const_ready")
        x_hi_ready, x_lo_ready = sem("x_hi_ready"), sem("x_lo_ready")
        w_hi_ready, w_lo_ready = sem("w_hi_ready"), sem("w_lo_ready")
        warm_ready = sem("warm_ready")
        wo_hi_ready = sem("wo_hi_ready")
        chunk_used = sem("chunk_used")
        acc_ready = sem("acc_ready")
        side_ready = sem("side_ready")
        acc_read = [sem(f"acc_read{i}") for i in range(4)]
        side_read = [sem(f"side_read{i}") for i in range(4)]
        trig_arg_ready, trig_ready = sem("trig_arg_ready"), sem("trig_ready")
        idx_split = sem("idx_split")
        relu_used = sem("relu_used")
        lat_ms_ready, lat_rs_ready = sem("lat_ms_ready"), sem("lat_rs_ready")
        lat_normed, lat_hi_ready = sem("lat_normed"), sem("lat_hi_ready")
        kpe_rotated, qpe_rotated = sem("kpe_rotated"), sem("qpe_rotated")
        q_step, q_rotated = sem("q_step"), sem("q_rotated")
        k_rotated = sem("k_rotated")
        a_hi_ready = sem("a_hi_ready")
        bias_ready = sem("bias_ready")
        scores_ready, masked_ready, probs_ready = sem("scores_ready"), sem("masked_ready"), sem("probs_ready")
        transposed, probsT_copied = sem("transposed"), sem("probsT_copied")
        pv_done = sem("pv_done")
        probsT_lo_ready = sem("probsT_lo_ready")
        vb_hi_ready, vb_lo_dve, vb_lo_pool = sem("vb_hi_ready"), sem("vb_lo_dve"), sem("vb_lo_pool")
        pair_read, pair_crossed, pair_merged = sem("pair_read"), sem("pair_crossed"), sem("pair_merged")
        rinv_ready, gate_scaled, obT_ready = sem("rinv_ready"), sem("gate_scaled"), sem("obT_ready")
        o_ps_read, o_ready = sem("o_ps_read"), sem("o_ready")
        oT_hi_ready, oT_lo_ready = sem("oT_hi_ready"), sem("oT_lo_ready")
        out_ps_ready, out_ps_read, y_ready = sem("out_ps_ready"), sem("out_ps_read"), sem("y_ready")
        var_ready, rstd_ready = sem("var_ready"), sem("rstd_ready")
        dve_step = sem("dve_step")

        block = ctx.enter_context(nc.Block())

        F_IQ, F_IK = 0, 2 * (TT - 1)
        F_LOGIT = F_IK + 1
        F_LAT = F_LOGIT + (TT - 1) * IDX_HEADS
        F_QT = F_LAT + QL_T + 1
        F_KT = F_QT + A_HEADS // 2
        F_END = F_KT + A_HEADS // 2
        A_QPE = NG * TT
        A_QN = A_QPE + TT
        A_KN = A_QN + 4
        A_VB = A_KN + 4
        A_END = A_VB + TT
        A_QPET, A_KPET = A_END + 2, A_END + 6

        def seen(n):
            return 2 * (n // 4)

        def last_seen(fills, bank):
            return seen([n for n in fills if n % 4 == bank][-1]) + 2

        ACC_LAST = [last_seen([*range(A_END), A_QPET, A_QPET + 1, A_KPET], b) for b in range(4)]
        SIDE_LAST = [last_seen(range(F_END), b) for b in range(4)]

        def wait_chunk_used(eng, c):
            g, k = divmod(c, KT)
            if k < KT - 1:
                eng.wait_ge(chunk_used, (KT - 1) * g + k + 1)
            else:
                eng.wait_ge(acc_ready, TT * (g + 1))

        def wait_tok(eng, g, m):
            eng.wait_ge(acc_read[m], 2 * (g + 1))

        def out_ps(i, b):
            bank = (ps_s[:, 0], ps_s[:, 1], ps_o[:, 0])[b] if i == TT - 1 else ps_y[:, b]
            return bank[:, 0:PIECES[i][b].stop - PIECES[i][b].start]

        def pair_done(g):
            return NU_A + 2 * (g + 1)

        def merge_pair(eng, g):
            eng.wait_ge(pair_crossed, 2 * (g + 1))
            if g % 4 == 0 and g > 0:
                eng.wait_ge(oT_lo_ready, 2 * (g // 4))
            for a in range(2):
                rows = slice(V_DIM * a, V_DIM * (a + 1))
                eng.tensor_tensor(obT[rows, g % 4], half_sum[rows, g % 2, a], crossed[rows, g % 2],
                                  ALU.add).then_inc(pair_merged, 1)
                if g >= POOL_PAIRS:
                    eng.wait_ge(pair_merged, 2 * g + a + 1)

        def wait_wo_hi(eng, j):
            if j < RING:
                eng.wait_ge(wo_hi_ready, j + 1)
            else:
                eng.wait_ge(w_hi_ready, C_OUT + j - RING + 1)

        @block.sync
        def _(sp):
            def load(q):
                if q >= RPAIR:
                    sp.wait_ge(w_lo_ready, 2 * (q - RPAIR) + 2)
                src, n = LOADS[q]
                s = 2 * (q % RPAIR)
                sp.dma_start(w_raw[:, s:s + 2, 0:n], src).then_inc(w_loaded[q % RPAIR], 16)

            xT_v = xT.rearrange("(k p) t -> p k t", p=P)
            for q, (a, b) in enumerate(((0, 1), (1, 2), (2, 4), (4, 6), (6, 8))):
                sp.dma_start(x_raw[:, a:b, :], xT_v[:, a:b, :]).then_inc(x_loaded[q], 16)
                if q >= 2:
                    load(q - 1)
                if q == 2:
                    sp.dma_start(pos_i[:, :], positions).then_inc(pos_loaded, 16)
                    sp.dma_start(freq_sb[:, :], freqs).then_inc(pos_loaded, 16)
            sp.dma_start(gq, q_norm_g).then_inc(norm_g_loaded, 16)
            sp.dma_start(gkv, kv_norm_g).then_inc(norm_g_loaded, 16)
            for q in range(RPAIR, C_OUT // 2):
                load(q)
            for n in range(F_KT, F_END):
                sp.wait_ge(side_read[n % 4], seen(n) + 2)
                h = 2 * (n - F_KT)
                for a in range(2):
                    sp.dma_start(kaT_swap[A_DIM * a:A_DIM * (a + 1), h:h + 2, :].bitcast(f32),
                                 kaT[A_DIM * (1 - a):A_DIM * (2 - a), h:h + 2, :].bitcast(f32)).then_inc(kaT_swapped, 16)
            sp.wait_ge(acc_ready, A_END + 2)
            for q in range(C_OUT // 2, C_OUT // 2 + RPAIR):
                load(q)
            sp.wait_ge(acc_read[2], ACC_LAST[2])
            sp.dma_start(kbT[NOPE:B_QK, 1:B_HEADS, :],
                         kbT[NOPE:B_QK, 0:1, :].broadcast_to([ROPE_D, B_HEADS - 1, SEQ])).then_inc(kpe_copied, 16)
            for q in range(C_OUT // 2 + RPAIR, len(LOADS)):
                load(q)
            sp.wait_ge(w_lo_ready, C_OUT + 2 * KT)
            sp.dma_start(lng[:, :], ln_g.broadcast_to([P, D_MODEL])).then_inc(ln_loaded, 16)
            sp.dma_start(lnb[:, :], ln_b.broadcast_to([P, D_MODEL])).then_inc(ln_loaded, 16)
            for i in range(2):
                m = ORDER[i]
                sp.dma_start(x_res[:, i, :], x[m * P:(m + 1) * P, :]).then_inc(xres_loaded[i], 16)
            for i, m in enumerate(ORDER):
                for b, cols in enumerate(PIECES[i]):
                    sp.wait_ge(y_ready, 2 * i + b + 1)
                    sp.dma_start(out[m * P:(m + 1) * P, cols], y_of(i)[:, cols]).then_inc(stored, 16)
                if i + 2 < TT:
                    m2 = ORDER[i + 2]
                    sp.dma_start(x_res[:, i, :], x[m2 * P:(m2 + 1) * P, :]).then_inc(xres_loaded[i], 16)
            sp.wait_ge(stored, 16 * sum(len(pieces) for pieces in PIECES))

        @block.gpsimd
        def _(pool):
            pool.memset(warm[:, :], 0.0).then_inc(warm_ready, 1)
            pool.memset(causal[:, :], 0.0).then_inc(const_ready, 1)
            pool.memset(ident[:, :], 0.0).then_inc(const_ready, 1)
            pool.memset(minus_half, -0.5).then_inc(const_ready, 1)
            pool.wait_ge(const_ready, 3)
            pool.affine_select(out=causal[:, :], in_=causal[:, :], compare_op=ALU.is_ge, fill=NEG,
                               base=SEQ - P, pattern=[[-1, SEQ]], channel_multiplier=1).then_inc(const_ready, 1)
            pool.affine_select(out=ident[:, :], in_=ident[:, :], compare_op=ALU.not_equal, fill=1.0,
                               base=0, pattern=[[-1, P]], channel_multiplier=1).then_inc(const_ready, 1)
            def rotate_queries(m):
                wait_tok(pool, G_Q, m)
                if m == 0:
                    pool.wait_ge(trig_ready, 1)
                    pool.wait_ge(relu_used, (TT - 1) * IDX_HEADS)
                src, t1, t2 = (v.rearrange("p (h a f) -> p h a f", a=2, f=FREQ_A)
                               for v in (q_tok[:, m, :], q_tmp[:, 0, :], q_tmp[:, 1, :]))
                cos, sin = (trig[:, j, m, 0:FREQ_A].unsqueeze(1).broadcast_to([P, A_HEADS, FREQ_A]) for j in (1, 0))
                if m > 0:
                    pool.wait_ge(q_rotated, 2 * m)
                for a in range(2):
                    pool.tensor_tensor(t1[:, :, a], src[:, :, a], cos, ALU.mult).then_inc(q_step, 1)
                    pool.tensor_tensor(t2[:, :, a], src[:, :, 1 - a], sin, ALU.mult).then_inc(q_step, 1)
                pool.wait_ge(q_step, 4 * (m + 1))
                pool.tensor_tensor(src[:, :, 0], t1[:, :, 0], t2[:, :, 0], ALU.subtract).then_inc(q_rotated, 1)
                pool.tensor_tensor(src[:, :, 1], t1[:, :, 1], t2[:, :, 1], ALU.add).then_inc(q_rotated, 1)

            for c in range(C_OUT):
                n, s = width(c), c % RING
                pool.wait_ge(w_loaded[(c // 2) % RPAIR], 16 * (c // 2 // RPAIR + 1))
                pool.wait_ge(w_hi_ready, c + 1)
                pool.tensor_tensor(w_lo[:, s, 0:n], w_raw[:, s, 0:n], w_hi[:, s, 0:n], ALU.subtract).then_inc(w_lo_ready, 1)
                if c == KT * (G_Q + 1) - 1:
                    pool.wait_ge(const_ready, 5)
                    pool.wait_ge(lat_ms_ready, 1)
                    pool.tensor_tensor(lat_r, lat_r, minus_half, ALU.pow).then_inc(lat_rs_ready, 1)
                if c in Q_ROTATE_AT:
                    rotate_queries(Q_ROTATE_AT.index(c))
            for m in range(TT):
                wait_tok(pool, A_QPE // TT, m)
                if m == 0:
                    pool.wait_ge(k_rotated, TT)
                else:
                    pool.wait_ge(qpe_rotated, 2 * m)
                n = B_HEADS * ROPE_D
                src, t1, t2 = (v.rearrange("p (h a f) -> p h a f", a=2, f=FREQ_B)
                               for v in (qpe_tok[:, m, :], tmp[:, 0, 0:n], tmp[:, 1, 0:n]))
                cos, sin = (trig[:, j, m, FREQ_A:NFREQ].unsqueeze(1).broadcast_to([P, B_HEADS, FREQ_B]) for j in (1, 0))
                for a in range(2):
                    pool.tensor_tensor(t1[:, :, a], src[:, :, a], cos, ALU.mult).then_inc(q_step, 1)
                    pool.tensor_tensor(t2[:, :, a], src[:, :, 1 - a], sin, ALU.mult).then_inc(q_step, 1)
                pool.wait_ge(q_step, 4 * (TT + m + 1))
                pool.tensor_tensor(src[:, :, 0], t1[:, :, 0], t2[:, :, 0], ALU.subtract).then_inc(qpe_rotated, 1)
                pool.tensor_tensor(src[:, :, 1], t1[:, :, 1], t2[:, :, 1], ALU.add).then_inc(qpe_rotated, 1)
            for j in (3, 2):
                pool.wait_ge(vb_hi_ready, VB_ORDER.index(j) + 1)
                pool.tensor_tensor(vb_parts[j][:, :, 1:3], vb[:, j, :].rearrange("p (q a d) -> p q a d", a=2, d=V_DIM),
                                   vb_parts[j][:, :, 0:4:3], ALU.subtract).then_inc(vb_lo_pool, 1)
            def scale_gate(i):
                m = ORDER[i]
                pool.wait_ge(rinv_ready, i + 1)
                wait_tok(pool, G_GB, m)
                g3 = gate[:, m, A_WIDTH:].rearrange("p (h d) -> p h d", h=HEADS)
                pool.tensor_tensor(g3, g3, rinv.unsqueeze(2).broadcast_to([P, HEADS, V_DIM]), ALU.mult).then_inc(gate_scaled, 1)

            for j in range(2 * KT):
                c = C_OUT + j
                pool.wait_ge(w_loaded[(c // 2) % RPAIR], 16 * (c // 2 // RPAIR + 1))
                wait_wo_hi(pool, j)
                if j == 0:
                    pool.wait_ge(scores_ready, NU_A)
                pool.tensor_tensor(wo_lo(j // 2, j % 2), w_raw[:, c % RING, :], wo_hi[:, j // 2, j % 2],
                                   ALU.subtract).then_inc(w_lo_ready, 1)
                if j == SCALE_AT:
                    scale_gate(0)

            def root(i):
                pool.wait_ge(var_ready, i + 1)
                pool.tensor_tensor(rstd, aggr[:, 2:3], minus_half[:, 0:1], ALU.pow).then_inc(rstd_ready, 1)

            scale_gate(1)
            for g in range(POOL_PAIRS, NPAIR):
                merge_pair(pool, g)
                if g == 9:
                    root(0)
                if g == 10:
                    scale_gate(2)
                if g == NPAIR - 3:
                    scale_gate(3)
                    root(1)
            root(2)
            root(3)

        @block.scalar
        def _(act):
            act.dma_start(w_raw[:, 0:2, 0:N_IDX], LOADS[0][0]).then_inc(w_loaded[0], 16)

            def split_hi(c):
                n, s = width(c), c % RING
                act.wait_ge(w_loaded[(c // 2) % RPAIR], 16 * (c // 2 // RPAIR + 1))
                if c >= C_OUT:
                    k, half = divmod(c - C_OUT, 2)
                    dst = wo_hi[:, k, half]
                else:
                    dst = w_hi[:, s, 0:n]
                    if c >= RING:
                        wait_chunk_used(act, c - RING)
                act.activation(dst, w_raw[:, s, 0:n], ACT.Copy).then_inc(w_hi_ready, 1)

            def evac_group(g):
                dst = {G_IDX: idx_tok, G_LAT: lat_tok, G_Q: q_tok, G_K: k_tok, G_V: va}.get(g, gate)
                off = A_WIDTH if g == G_GB else 0
                n = GROUPS[g][1]
                if g == G_GA:
                    act.wait_ge(relu_used, (TT - 1) * IDX_HEADS)
                    act.wait_ge(kpe_rotated, TT)
                    act.wait_ge(side_ready, F_LAT + QL_T + 1)
                for m in range(TT):
                    act.wait_ge(acc_ready, TT * g + m + 1)
                    act.activation(dst[:, m, off:off + n], acc[:, m, 0:n],
                                   ACT.Silu if g in (G_GA, G_GB) else ACT.Copy).then_inc(acc_read[m], 2)

            for k in range(KT):
                act.wait_ge(x_loaded[k if k < 2 else 1 + k // 2], 16)
                act.activation(x_hi[:, k, :], x_raw[:, k, :], ACT.Copy).then_inc(x_hi_ready, 1)
                split_hi(k)

            def evac_idxT(n):
                act.wait_ge(side_ready, n + 1)
                if n < F_IK:
                    m, quad = divmod(n, 2)
                    dst = iqT[:, 4 * quad:4 * quad + 4, m * P:(m + 1) * P]
                else:
                    dst = ikT[:, :].rearrange("p (a b) -> p a b", a=4)
                act.activation(dst, side[:, n % 4].rearrange("p (a b) -> p a b", a=4), ACT.Copy).then_inc(side_read[n % 4], 2)

            def relu_unit(i):
                n, N = F_LOGIT + i, (2 + i // IDX_HEADS) * P
                act.wait_ge(side_ready, n + 1)
                if i >= 4:
                    act.wait_ge(relu_used, i - 3)
                act.activation(relu[:, i % 4, 0:N], side[:, n % 4, 0:N], ACT.Relu, scale=IDX_DIM ** -0.5).then_inc(side_read[n % 4], 2)

            def evac_lat_hi():
                act.wait_ge(norm_g_loaded, 32)
                for t in range(QL_T + 1):
                    n = F_LAT + t
                    act.wait_ge(side_ready, n + 1)
                    act.activation(latT_hi[:, t, :], side[:, n % 4], ACT.Copy,
                                   scale=gq[:, t:t + 1] if t < QL_T else gkv).then_inc(lat_hi_ready, 1)

            def high_parts(first, i):
                dst, n = (qaT if first == F_QT else kaT), first + i
                act.wait_ge(side_ready, n + 1)
                for a in range(2):
                    rows = slice(A_DIM * a, A_DIM * (a + 1))
                    act.activation(dst[rows, 2 * i + a, :], side[rows, n % 4], ACT.Copy).then_inc(a_hi_ready, 1)

            for g in range(NG):
                nxt = KT * (g + 1)
                for j in range(KT - 1):
                    if nxt + j < C_OUT and not (g == G_IDX and j == KT - 2):
                        split_hi(nxt + j)
                    if g == G_IDX and j == 2:
                        act.wait_ge(trig_arg_ready, 1)
                        act.activation(trig[:, :, :, :].rearrange("p a t f -> p (a t f)"), trig_tmp[:, 0, :],
                                       ACT.Sin).then_inc(trig_ready, 1)
                    if g == G_Q:
                        if j == 0:
                            for n in range(4):
                                evac_idxT(n)
                        elif j == 1:
                            for n in range(4, F_LOGIT):
                                evac_idxT(n)
                        else:
                            for i in range(4 * (j - 2), 4 * (j - 1)):
                                relu_unit(i)
                    if g == G_GA and j >= QT_AT:
                        high_parts(F_QT, j - QT_AT)
                    if g == G_GB and j >= KT_AT:
                        high_parts(F_KT, j - KT_AT)
                evac_group(g)
                if g == G_Q:
                    for i in range(4 * (KT - 3), 4 * (KT - 2)):
                        relu_unit(i)
                if g == G_V:
                    evac_lat_hi()
                if g == G_GA:
                    for i in range(KT - 1 - QT_AT, A_HEADS // 2):
                        high_parts(F_QT, i)
                if g == G_GB:
                    for i in range(KT - 1 - KT_AT, A_HEADS // 2):
                        high_parts(F_KT, i)
                for c in range(nxt + KT - (2 if g == G_IDX else 1), min(nxt + KT, C_OUT)):
                    split_hi(c)

            for m in range(TT):
                act.wait_ge(acc_ready, A_QPE + m + 1)
                act.activation(qpe_tok[:, m, :], acc[:, m, 0:B_HEADS * ROPE_D], ACT.Copy).then_inc(acc_read[m], 2)
            act.wait_ge(const_ready, 5)
            act.activation(unused, minus_half[:, 0:1], ACT.Exp)
            def evac_qpeT(j):
                quad, r = divmod(j, 2)
                act.wait_ge(acc_ready, A_END + quad + 1)
                ins = act.activation(qbT[NOPE:B_QK, 4 * quad + r, :], ps_y[32 * r:32 * r + 32, quad], ACT.Copy)
                if r == 1:
                    ins.then_inc(acc_read[2 + quad], 1)

            def exp_unit(u):
                N = unit(u)[3]
                act.wait_ge(masked_ready, u + 1)
                act.activation(probs[:, u % NPROBS, 0:N], probs[:, u % NPROBS, 0:N], ACT.Exp, bias=neg_max[:, u % 8:u % 8 + 1],
                               scale=-1.0, accum_out=row_sum[:, u:u + 1]).then_inc(probs_ready, 1)

            for first, dst in ((A_QN, qbT), (A_KN, kbT)):
                for p in range(4):
                    act.wait_ge(acc_ready, first + p + 1)
                    act.activation(dst[0:NOPE, 2 * p, :], acc[0:NOPE, p], ACT.Copy).then_inc(acc_read[p], 1)
                if first == A_QN:
                    for u in range(2):
                        exp_unit(u)
            for m in range(TT):
                act.wait_ge(acc_ready, A_VB + m + 1)
                act.activation(vb[:, m, :], acc[:, m], ACT.Copy).then_inc(acc_read[m], 2)

            def copy_probsT(u):
                N = unit(u)[3]
                act.wait_ge(transposed, slot_of[u] + 1)
                if u >= 3:
                    act.wait_ge(pv_done, u - 2)
                dst = probsT[:, u % 3, 0:N] if u < NU_A else probsT_b[:, u % 3, 0, 0:N]
                act.activation(dst, ps_pT[:, slot_of[u] % 2, 0:N], ACT.Copy).then_inc(probsT_copied, 1)

            def copy_oT_hi(i, b):
                n = slot_of[i, b]
                if i >= 2 and b == 0:
                    act.wait_ge(out_ps_ready, 2 * (i - 1))
                if b == 0:
                    act.wait_ge(transposed, n + 1)
                    src = ps_pT[:, n % 2].rearrange("p (a b) -> p a b", a=4)
                else:
                    act.wait_ge(obT_ready, i + 1)
                    src = obT[:, :, :]
                act.activation((oT0, oT1)[i % 2][:, 0, 4 * b:4 * b + 4, :], src, ACT.Copy).then_inc(oT_hi_ready, 1)

            def vb_high(n):
                j = VB_ORDER[n]
                if n == 1:
                    act.wait_ge(scores_ready, NU_A)
                    act.wait_ge(masked_ready, NU_A)
                if j == 2:
                    act.wait_ge(vb_lo_dve, 2)
                act.activation(vb_parts[j][:, :, 0:4:3], vb[:, j, :].rearrange("p (q a d) -> p q a d", a=2, d=V_DIM),
                               ACT.Copy).then_inc(vb_hi_ready, 1)

            def cross_pair(g):
                act.wait_ge(pair_read, g + 1)
                if g >= 2:
                    act.wait_ge(pair_merged, 2 * (g - 1))
                act.activation(crossed[0:V_DIM, g % 2], half_sum[V_DIM:P, g % 2, 0], ACT.Copy).then_inc(pair_crossed, 1)
                act.activation(crossed[V_DIM:P, g % 2], half_sum[0:V_DIM, g % 2, 1], ACT.Copy).then_inc(pair_crossed, 1)

            for u in range(NU + T_LAG):
                if u >= T_LAG:
                    copy_probsT(u - T_LAG)
                i, j = divmod(u - NU_A, HEADS)
                if 0 < i < TT and j == OT_AT:
                    copy_oT_hi(i - 1, 0)
                if 0 < i < TT and j == OT_AT + 2:
                    copy_oT_hi(i - 1, 1)
                g = PAIR_AT.get(u - 1)
                if g is not None:
                    cross_pair(g)
                if 2 <= u < NU:
                    exp_unit(u)
                if 0 <= u - PET_AT - 1 < 4:
                    evac_qpeT(u - PET_AT - 1)
                if u == PET_AT + 7:
                    act.wait_ge(acc_ready, A_END + 3)
                    act.activation(kbT[NOPE:B_QK, 0, :], ps_y[0:ROPE_D, 0], ACT.Copy).then_inc(acc_read[2], 2)
                if 0 <= u - WO_LATE < RING:
                    split_hi(C_OUT + RING + u - WO_LATE)
                if u == VB_EARLY:
                    vb_high(0)
                if u == NU_A:
                    vb_high(1)
                    vb_high(2)
                if u == NU_A + 1:
                    vb_high(3)
            for g in range(NPAIR - PAIRS_LATE, NPAIR):
                cross_pair(g)
            copy_oT_hi(TT - 1, 0)
            copy_oT_hi(TT - 1, 1)

        @block.vector
        def _(dve):
            count = [0]

            def step(ins):
                ins.then_inc(dve_step, 1)
                count[0] += 1
                return count[0]

            def after(ins):
                dve.wait_ge(dve_step, step(ins))

            V = nc.vector

            def x_low(k):
                dve.wait_ge(x_loaded[k if k < 2 else 1 + k // 2], 16)
                dve.wait_ge(x_hi_ready, k + 1)
                V.tensor_tensor(x_lo[:, k, :], x_raw[:, k, :], x_hi[:, k, :], ALU.subtract).then_inc(x_lo_ready, 1)

            for k in range(4):
                x_low(k)

            nt = TT * NFREQ
            ang, turns = trig_tmp[:, 0, :], trig_tmp[:, 1, :]
            ROUND = 1.5 * 2 ** 23
            two_pi = 2 * np.pi
            C1 = 6.28125
            C2 = float(np.round((two_pi - C1) * 2 ** 20) / 2 ** 20)
            C3 = float(two_pi - C1 - C2)
            dve.wait_ge(pos_loaded, 32)
            after(V.tensor_copy(pos_f, pos_i[:, :]))
            for half in range(2):
                dst = ang[:, half * nt:(half + 1) * nt].rearrange("p (t f) -> p t f", t=TT)
                last = step(V.tensor_tensor(dst, pos_f.unsqueeze(2).broadcast_to([P, TT, NFREQ]),
                                            freq_sb[:, :].unsqueeze(1).broadcast_to([P, TT, NFREQ]), ALU.mult))
            dve.wait_ge(dve_step, last)
            for half in range(2):
                s = slice(half * nt, (half + 1) * nt)
                last = step(V.tensor_scalar(turns[:, s], ang[:, s], float(1 / two_pi), 0.25 * half, ALU.mult, ALU.add))
            x_low(4)
            dve.wait_ge(dve_step, last)
            after(V.tensor_scalar(turns, turns, ROUND, ROUND, ALU.add, ALU.subtract))
            x_low(5)
            for c in (C1, C2, C3):
                after(V.scalar_tensor_tensor(out=ang, in0=turns, scalar=-c, in1=ang, op0=ALU.mult, op1=ALU.add))
            x_low(6)
            after(V.tensor_scalar(ang[:, nt:], ang[:, nt:], float(np.pi / 2), None, ALU.add))
            x_low(7)
            V.tensor_scalar(ang, ang, 3.1415925, -3.1415925, ALU.min, ALU.max).then_inc(trig_arg_ready, 1)

            def rope(dst, src, m, heads, half, f0, wait=None):
                n = heads * 2 * half
                s4 = src.rearrange("p (h a f) -> p h a f", a=2, f=half)
                d4 = dst.rearrange("p (h a f) -> p h a f", a=2, f=half)
                t1 = tmp[:, 0, 0:n].rearrange("p (h a f) -> p h a f", a=2, f=half)
                t2 = tmp[:, 1, 0:n].rearrange("p (h a f) -> p h a f", a=2, f=half)
                cos = trig[:, 1, m, f0:f0 + half].unsqueeze(1).broadcast_to([P, heads, half])
                sin = trig[:, 0, m, f0:f0 + half].unsqueeze(1).broadcast_to([P, heads, half])
                for a in range(2):
                    step(V.tensor_tensor(t1[:, :, a], s4[:, :, a], cos, ALU.mult))
                    last = step(V.tensor_tensor(t2[:, :, a], s4[:, :, 1 - a], sin, ALU.mult))
                dve.wait_ge(dve_step, last)
                step(V.tensor_tensor(d4[:, :, 0], t1[:, :, 0], t2[:, :, 0], ALU.subtract))
                after(V.tensor_tensor(d4[:, :, 1], t1[:, :, 1], t2[:, :, 1], ALU.add))

            nrot = (IDX_HEADS + 1) * IDX_DIM
            dve.wait_ge(trig_ready, 1)
            for m in range(TT):
                wait_tok(dve, G_IDX, m)
            for k in range(2):
                dve.wait_ge((x_hi_ready, x_lo_ready)[k], KT)
            step(V.tensor_scalar(iw.rearrange("p (t h) -> p t h", t=TT), idx_tok[:, :, nrot:N_IDX],
                                 IDX_HEADS ** -0.5, None, ALU.mult))
            for m in range(TT):
                rope(idx_tok[:, m, 0:nrot], idx_tok[:, m, 0:nrot], m, IDX_HEADS + 1, FREQ_B, FREQ_A)
                q3 = idx_tok[:, m, 0:IDX_HEADS * IDX_DIM].rearrange("p (h d) -> p h d", d=IDX_DIM)
                k2 = idx_tok[:, m, IDX_HEADS * IDX_DIM:nrot]
                k3 = k2.unsqueeze(1).broadcast_to([P, 2, IDX_DIM])
                if m > 0:
                    st = iq_st[:, m - 1]
                    for a in (0, 2):
                        last = step(V.tensor_copy(st[:, :, a].bitcast(f32r), q3))
                kst = ik_st[:, m]
                last = step(V.tensor_copy(kst[:, 0:2].bitcast(f32r), k3))
                dve.wait_ge(dve_step, last)
                if m > 0:
                    for a in (1, 3):
                        last = step(V.tensor_tensor(st[:, :, a].bitcast(f32r), q3, st[:, :, 0], ALU.subtract))
                V.tensor_tensor(kst[:, 2:4].bitcast(f32r), k3, kst[:, 0:2], ALU.subtract).then_inc(idx_split, 1)

            dve.wait_ge(idx_split, TT)
            for m in range(TT):
                wait_tok(dve, G_LAT, m)
                for j, (a, b) in enumerate(((0, Q_LORA), (Q_LORA, Q_LORA + KV_LORA))):
                    src = lat_tok[:, m, a:b]
                    last = step(V.tensor_tensor_reduce(out=tmp[:, m % 2, a:b], in0=src, in1=src, scale=1.0, scalar=0.0,
                                                       op0=ALU.mult, op1=ALU.add, accum_out=ssq[:, 2 * m + j:2 * m + j + 1]))
                dve.wait_ge(dve_step, last)
            ssq2, lat_r2 = (v.rearrange("p (t j) -> p t j", j=2) for v in (ssq, lat_r))
            for j, n in enumerate((Q_LORA, KV_LORA)):
                last = step(V.tensor_scalar(lat_r2[:, :, j], ssq2[:, :, j], 1.0 / n, RMS_EPS, ALU.mult, ALU.add))
            dve.wait_ge(dve_step, last)
            dve.sem_inc(lat_ms_ready, 1)
            dve.wait_ge(lat_rs_ready, 1)
            for m in range(TT):
                for j, (a, b) in enumerate(((0, Q_LORA), (Q_LORA, Q_LORA + KV_LORA))):
                    last = V.tensor_scalar(lat_tok[:, m, a:b], lat_tok[:, m, a:b], lat_r[:, 2 * m + j:2 * m + j + 1],
                                           None, ALU.mult).then_inc(lat_normed, 1)
            for m in range(TT):
                rope(kpe_tok[:, m, :], lat_tok[:, m, Q_LORA + KV_LORA:N_LAT], m, 1, FREQ_B, FREQ_A)
                dve.sem_inc(kpe_rotated, 1)

            dve.wait_ge(const_ready, 5)
            for i in range((TT - 1) * IDX_HEADS):
                m, h = 1 + i // IDX_HEADS, i % IDX_HEADS
                N = (m + 1) * P
                sc = score[:, SCORE_AT[m]:SCORE_AT[m] + N]
                n = F_LOGIT + i
                dve.wait_ge(side_read[n % 4], seen(n) + 2)
                if h > 0:
                    dve.wait_ge(relu_used, i)
                V.scalar_tensor_tensor(out=sc, in0=relu[:, i % 4, 0:N], scalar=iw[:, m * IDX_HEADS + h:m * IDX_HEADS + h + 1],
                                       in1=causal[:, SEQ - N:SEQ] if h == 0 else sc, op0=ALU.mult,
                                       op1=ALU.add).then_inc(relu_used, 1)
            dve.wait_ge(relu_used, (TT - 1) * IDX_HEADS)

            spans = [score[:, SCORE_AT[m]:SCORE_AT[m] + (m + 1) * P] for m in range(1, TT)]
            for r in range(TOP_K // 8):
                for j, sc in enumerate(spans):
                    if r > 0:
                        dve.wait_ge(dve_step, count[0] - 2)
                    step(V.max(top8[:, 8 * j:8 * j + 8], sc))
                for j, sc in enumerate(spans):
                    dve.wait_ge(dve_step, count[0] - 2)
                    step(V.match_replace(out=sc, in_to_replace=top8[:, 8 * j:8 * j + 8], in_values=sc, imm_value=TAKEN))
            dve.wait_ge(dve_step, count[0])
            V.tensor_scalar(score[:, :], score[:, :], TAKEN, NEG, ALU.not_equal, ALU.mult).then_inc(bias_ready, 1)

            for t in range(QL_T + 1):
                n = F_LAT + t
                dve.wait_ge(lat_hi_ready, t + 1)
                V.scalar_tensor_tensor(out=latT_lo[:, t, :], in0=side[:, n % 4], scalar=gq[:, t:t + 1] if t < QL_T else gkv,
                                       in1=latT_hi[:, t, :], op0=ALU.mult, op1=ALU.subtract).then_inc(side_read[n % 4], 2)

            for m in range(TT):
                wait_tok(dve, G_K, m)
                rope(k_tok[:, m, :], k_tok[:, m, :], m, A_HEADS, FREQ_A, 0)
                dve.sem_inc(k_rotated, 1)

            for first, dst in ((F_QT, qaT), (F_KT, kaT)):
                for h in range(A_HEADS):
                    n, a = first + h // 2, h % 2
                    rows, low = slice(A_DIM * a, A_DIM * (a + 1)), slice(A_DIM * (1 - a), A_DIM * (2 - a))
                    dve.wait_ge(a_hi_ready, 2 * (n - F_QT) + a + 1)
                    ins = V.tensor_tensor(dst[low, h, :], side[rows, n % 4], dst[rows, h, :], ALU.subtract)
                    if a == 1:
                        ins.then_inc(side_read[n % 4], 2)

            def evac_qpeT(j):
                quad, r = divmod(j, 2)
                dve.wait_ge(acc_ready, A_END + quad + 1)
                ins = V.tensor_copy(qbT[NOPE:B_QK, 4 * quad + 2 + r, :], ps_y[64 + 32 * r:96 + 32 * r, quad])
                if r == 1:
                    ins.then_inc(acc_read[2 + quad], 1)

            def mask_unit(u):
                v, m, h, N = unit(u)
                a = v < TT
                bias = spans[m - 1] if a and m > 0 else causal[:, SEQ - N:SEQ]
                scale = (A_DIM if a else B_QK) ** -0.5
                dve.wait_ge(scores_ready, u + 1)
                if u == 0:
                    dve.wait_ge(bias_ready, 1)
                if u >= NPROBS:
                    dve.wait_ge(transposed, slot_of[u - NPROBS] + 1)
                V.tensor_tensor_reduce(out=probs[:, u % NPROBS, 0:N], in0=ps_s[:, u % 2, 0:N], in1=bias, scale=-scale,
                                       scalar=3.0e38, op0=ALU.add, op1=ALU.min,
                                       accum_out=neg_max[:, u % 8:u % 8 + 1]).then_inc(masked_ready, 1)

            for first, dst in ((A_QN, qbT), (A_KN, kbT)):
                for p in range(4):
                    dve.wait_ge(acc_ready, first + p + 1)
                    V.tensor_copy(dst[0:NOPE, 2 * p + 1, :], acc[NOPE:P, p]).then_inc(acc_read[p], 1)
                if first == A_QN:
                    for u in range(2):
                        mask_unit(u)

            def normalise(v):
                dve.wait_ge(pv_done, HEADS * (v + 1))
                after(V.reciprocal(rinv, row_sum[:, HEADS * v:HEADS * (v + 1)]))
                V.tensor_tensor(o_norm[:, :].rearrange("p (h d) -> p h d", h=HEADS),
                                ps_o[:, v % 2].rearrange("p (h d) -> p h d", h=HEADS),
                                rinv.unsqueeze(2).broadcast_to([P, HEADS, A_DIM]), ALU.mult).then_inc(o_ps_read, 1)

            def apply_gate(v):
                m = ORDER[v % TT]
                cols = slice(A_WIDTH * (v // TT), A_WIDTH * (v // TT + 1))
                dve.wait_ge(o_ps_read, v + 1)
                wait_tok(dve, G_GA, m)
                V.tensor_tensor(gate[:, m, cols], o_norm[:, :], gate[:, m, cols], ALU.mult).then_inc(o_ready, 1)

            def copy_oT_lo(i, b):
                dst = (oT0, oT1)[i % 2]
                dve.wait_ge(oT_hi_ready, 2 * i + b + 1)
                src = ps_pT[:, slot_of[i, b] % 2].rearrange("p (a b) -> p a b", a=4) if b == 0 else obT[:, :, :]
                V.tensor_tensor(dst[:, 1, 4 * b:4 * b + 4, :], src, dst[:, 0, 4 * b:4 * b + 4, :],
                                ALU.subtract).then_inc(oT_lo_ready, 1)

            def probs_low(u):
                N, w = unit(u)[3], u % 3
                dve.wait_ge(probsT_copied, u + 1)
                V.tensor_tensor(probsT_b[:, w, 1, 0:N], ps_pT[:, slot_of[u] % 2, 0:N], probsT_b[:, w, 0, 0:N],
                                ALU.subtract).then_inc(probsT_lo_ready, 1)

            def vb_low(n):
                j = VB_ORDER[n]
                dve.wait_ge(vb_hi_ready, n + 1)
                V.tensor_tensor(vb_parts[j][:, :, 1:3], vb[:, j, :].rearrange("p (q a d) -> p q a d", a=2, d=V_DIM),
                                vb_parts[j][:, :, 0:4:3], ALU.subtract).then_inc(vb_lo_dve, 1)

            def read_pair(g):
                dve.wait_ge(pv_done, pair_done(g))
                bank = ps_o[:, g % 2].rearrange("p (h a t) -> p h t a", h=2, a=2)
                if g >= 2:
                    dve.wait_ge(pair_merged, 2 * (g - 1))
                V.tensor_reduce(half_sum[:, g % 2], bank, mybir.AxisListType.X, ALU.add).then_inc(pair_read, 1)

            def row_sums(v):
                dve.wait_ge(probs_ready, HEADS * (v + 1))
                if v > TT:
                    dve.wait_ge(gate_scaled, v - TT)
                V.reciprocal(rinv, row_sum[:, HEADS * v:HEADS * (v + 1)]).then_inc(rinv_ready, 1)

            def gate_obT(i):
                n = slot_of[i, 1]
                dve.wait_ge(transposed, n + 1)
                dve.wait_ge(pair_merged, 8 * (i + 1))
                V.tensor_tensor(obT[:, :, :], obT[:, :, :], ps_pT[:, n % 2].rearrange("p (a b) -> p a b", a=4),
                                ALU.mult).then_inc(obT_ready, 1)

            def wo_high(j):
                c = C_OUT + j
                dve.wait_ge(w_loaded[(c // 2) % RPAIR], 16 * (c // 2 // RPAIR + 1))
                if j == 0:
                    dve.wait_ge(acc_ready, A_END)
                V.tensor_copy(wo_hi[:, j // 2, j % 2], w_raw[:, c % RING, :]).then_inc(wo_hi_ready, 1)

            def ln_residual(i, b):
                cols, v = PIECES[i][b], y_of(i)
                src = out_ps(i, b)
                if b == 0:
                    dve.wait_ge(xres_loaded[i % 2], 16 * (i // 2 + 1))
                    if 0 < i < TT - 1:
                        dve.wait_ge(stored, 32 * i)
                dve.wait_ge(out_ps_ready, 2 * i + b + 1)
                V.scalar_tensor_tensor(out=v[:, cols], in0=x_res[:, i % 2, cols], scalar=ALPHA, in1=src,
                                       op0=ALU.mult, op1=ALU.add).then_inc(out_ps_read, 1)
                dve.wait_ge(out_ps_read, 2 * i + b + 1)
                n = BANK if i < TT - 1 else BANK // 2
                for a in range(cols.start // n, cols.stop // n):
                    step(V.bn_stats(stats[:, 6 * a:6 * a + 6], v[:, a * n:(a + 1) * n]))

            def ln_stats(i):
                dve.wait_ge(dve_step, count[0])
                after(V.bn_aggr(aggr[:, 0:2], stats[:, 0:12 if i < TT - 1 else 24]))
                V.tensor_scalar(aggr[:, 2:3], aggr[:, 1:2], LN_EPS, None, ALU.add).then_inc(var_ready, 1)

            def ln_centre(i, b):
                cols, v = PIECES[i][b], y_of(i)
                if i == 0 and b == 0:
                    dve.wait_ge(ln_loaded, 32)
                step(V.scalar_tensor_tensor(out=v[:, cols], in0=v[:, cols], scalar=aggr[:, 0:1], in1=lng[:, cols],
                                            op0=ALU.subtract, op1=ALU.mult))

            def ln_scale(i, b):
                cols, v = PIECES[i][b], y_of(i)
                dve.wait_ge(dve_step, count[0])
                dve.wait_ge(rstd_ready, i + 1)
                V.scalar_tensor_tensor(out=v[:, cols], in0=v[:, cols], scalar=rstd, in1=lnb[:, cols],
                                       op0=ALU.mult, op1=ALU.add).then_inc(y_ready, 1)

            def ln_schedule(t):
                u = OUT_AT[t]
                return [(u + 6, lambda: ln_residual(t, 0)), (u + 8, lambda: ln_residual(t, 1)), (u + 9, lambda: ln_stats(t)),
                        (u + 9, lambda: ln_centre(t, 0)), (u + 10, lambda: ln_centre(t, 1)),
                        (u + 10, lambda: ln_scale(t, 0)), (u + 11, lambda: ln_scale(t, 1))]

            for u in range(NU):
                if u >= 2:
                    mask_unit(u)
                if u - T_LAG >= NU_A:
                    probs_low(u - T_LAG)
                if u == NU_A + 1:
                    vb_low(1)
                    vb_low(2)
                v, j = divmod(u, HEADS)
                i = v - TT
                if 0 < v <= TT and j == PV_LAG:
                    normalise(v - 1)
                if 0 < v <= TT and j == PV_LAG + 1:
                    apply_gate(v - 1)
                if v > TT and j == 2:
                    row_sums(v - 1)
                if 0 <= u - PET_AT - 1 < 4:
                    evac_qpeT(u - PET_AT - 1)
                if 0 <= u - WO_EARLY < RING:
                    wo_high(u - WO_EARLY)
                if 0 < i and j == OT_AT:
                    copy_oT_lo(i - 1, 0)
                if 0 < i and j == OT_AT + 1:
                    gate_obT(i - 1)
                if 0 < i and j == OT_AT + 2:
                    copy_oT_lo(i - 1, 1)
                if u in PAIR_AT:
                    read_pair(PAIR_AT[u])
                if u - 1 in PAIR_AT and PAIR_AT[u - 1] < POOL_PAIRS:
                    merge_pair(V, PAIR_AT[u - 1])
                for t in range(TT - 2):
                    for at_u, take in ln_schedule(t):
                        if at_u == u:
                            take()
            late = [take for at_u, take in ln_schedule(TT - 3) if at_u >= NU]
            probs_low(NU - 2)
            read_pair(NPAIR - 3)
            probs_low(NU - 1)
            row_sums(NPASS - 1)
            for take in late[:-2]:
                take()
            read_pair(NPAIR - 2)
            for take in late[-2:]:
                take()
            read_pair(NPAIR - 1)
            copy_oT_lo(TT - 1, 0)
            gate_obT(TT - 1)
            copy_oT_lo(TT - 1, 1)
            for t in range(TT - 2, TT):
                pieces = range(len(PIECES[t]))
                for b in pieces:
                    ln_residual(t, b)
                ln_stats(t)
                for b in pieces:
                    ln_centre(t, b)
                for b in pieces:
                    ln_scale(t, b)

        @block.tensor
        def _(pe):
            mm = nc.tensor.matmul

            def products(dst, pairs, start, stop):
                for j, (a, b) in enumerate(pairs):
                    ins = mm(dst, a, b, start=start and j == 0, stop=stop and j == len(pairs) - 1)
                return ins

            def group(g, beside=None):
                n = GROUPS[g][1]
                for k in range(KT):
                    c = KT * g + k
                    s = c % RING
                    if c == 0:
                        pe.wait_ge(x_hi_ready, 1)
                        pe.wait_ge(w_hi_ready, 1)
                        for j, (xp, wp) in enumerate(((x_hi, w_hi), (x_lo, w_hi), (x_hi, w_lo))):
                            if j > 0:
                                pe.wait_ge((x_lo_ready, w_lo_ready)[j - 1], 1)
                            for m in range(TT):
                                ins = mm(acc[:, m, 0:n], xp[:, 0, m * P:(m + 1) * P], wp[:, 0, 0:n], start=j == 0, stop=False)
                        ins.then_inc(chunk_used, 1)
                        continue
                    if g == 0:
                        pe.wait_ge(x_hi_ready, k + 1)
                        pe.wait_ge(x_lo_ready, k + 1)
                    pe.wait_ge(w_hi_ready, c + 1)
                    pe.wait_ge(w_lo_ready, c + 1)
                    for m in range(TT):
                        if k == 0 and g > 0:
                            pe.wait_ge(acc_read[m], 2 * g)
                        t = slice(m * P, (m + 1) * P)
                        wh, wl = w_hi[:, s, 0:n], w_lo[:, s, 0:n]
                        ins = products(acc[:, m, 0:n], ((x_hi[:, k, t], wh), (x_hi[:, k, t], wl), (x_lo[:, k, t], wh)),
                                       k == 0, k == KT - 1)
                        if k == KT - 1:
                            ins.then_inc(acc_ready, 1)
                        elif m == TT - 1:
                            ins.then_inc(chunk_used, 1)
                    if beside:
                        beside(g, k)

            def fill(n):
                if n >= 4:
                    pe.wait_ge(side_read[n % 4], seen(n))
                return side[:, n % 4]

            def idx_transposes(n):
                if n == 0:
                    pe.wait_ge(idx_split, TT)
                    pe.wait_ge(const_ready, 5)
                bank = fill(n)
                for j in range(4):
                    if n < F_IK:
                        m, quad = divmod(n, 2)
                        src = iq_st[:, m, 4 * quad + j].rearrange("p a d -> p (a d)")
                    else:
                        src = ik_st[:, j].rearrange("p a d -> p (a d)")
                    ins = nc.tensor.transpose(bank[:, j * P:(j + 1) * P], src, ident[:, :])
                ins.then_inc(side_ready, 1)

            def idx_logits(i):
                m, h = 1 + i // IDX_HEADS, i % IDX_HEADS
                N = (m + 1) * P
                bank = fill(F_LOGIT + i)
                if i == 0:
                    for n in range(F_IK - 3, F_IK + 1):
                        pe.wait_ge(side_read[n % 4], seen(n) + 2)
                mm(bank[:, 0:N], iqT[:, h, (m - 1) * P:m * P], ikT[:, 0:N], start=True, stop=True).then_inc(side_ready, 1)

            def lat_transposes():
                pe.wait_ge(lat_normed, 2 * TT)
                for t in range(QL_T + 1):
                    bank = fill(F_LAT + t)
                    for m in range(TT):
                        ins = nc.tensor.transpose(bank[:, m * P:(m + 1) * P], lat_tok[:, m, t * P:(t + 1) * P], ident[:, :])
                    ins.then_inc(side_ready, 1)

            def a_transposes(first, i):
                src, bank = (q_tok if first == F_QT else k_tok), fill(first + i)
                for m in range(TT):
                    if i == 0:
                        if first == F_QT:
                            pe.wait_ge(q_rotated, 2 * (m + 1))
                        else:
                            pe.wait_ge(k_rotated, m + 1)
                    ins = nc.tensor.transpose(bank[:, m * P:(m + 1) * P], src[:, m, i * P:(i + 1) * P], ident[:, :])
                ins.then_inc(side_ready, 1)

            def beside(g, k):
                if g == G_Q:
                    if k < 2:
                        for n in range(4 * k, min(4 * k + 4, F_LOGIT)):
                            idx_transposes(n)
                    else:
                        for i in range(4 * (k - 2), 4 * (k - 1)):
                            idx_logits(i)
                if g == G_V and k == KT - 1:
                    lat_transposes()
                if g == G_GA and k >= QT_AT:
                    a_transposes(F_QT, k - QT_AT)
                if g == G_GB and k >= KT_AT:
                    a_transposes(F_KT, k - KT_AT)

            pe.wait_ge(warm_ready, 1)
            for _ in range(NWARM):
                mm(side[:, 0, 0:P], warm[:, :], warm[:, :], start=True, stop=True)
            for g in range(NG):
                group(g, beside)

            def wait_chunk(c):
                pe.wait_ge(w_hi_ready, c + 1)
                pe.wait_ge(w_lo_ready, c + 1)

            for n in range(F_LAT, F_LAT + QL_T + 1):
                pe.wait_ge(side_read[n % 4], seen(n) + 2)
            npe = B_HEADS * ROPE_D
            wait_chunk(C_UQP + 1)
            for m in range(TT):
                pe.wait_ge(acc_read[m], seen(A_QPE + m))
                t0 = slice(m * P, (m + 1) * P)
                for t in range(QL_T):
                    s = (C_UQP + t) % RING
                    ins = products(acc[:, m, 0:npe], ((latT_hi[:, t, t0], w_hi[:, s, 0:npe]), (latT_hi[:, t, t0], w_lo[:, s, 0:npe]),
                                                      (latT_lo[:, t, t0], w_hi[:, s, 0:npe])), t == 0, t == QL_T - 1)
                ins.then_inc(acc_ready, 1)
            for p in range(4):
                pe.wait_ge(acc_read[p], seen(A_QN + p))
                for t in range(QL_T):
                    s, cols = (C_UQN + t) % RING, slice(p * P, (p + 1) * P)
                    ins = products(acc[:, p], ((w_hi[:, s, cols], latT_hi[:, t, :]), (w_hi[:, s, cols], latT_lo[:, t, :]),
                                               (w_lo[:, s, cols], latT_hi[:, t, :])), t == 0, t == QL_T - 1)
                ins.then_inc(acc_ready, 1)
            def scores(u):
                v, m, h, N = unit(u)
                b = u % 2
                if u < 2:
                    pe.wait_ge(side_read[b], SIDE_LAST[b])
                else:
                    pe.wait_ge(masked_ready, u - 1)
                t = slice(m * P, (m + 1) * P)
                if v < TT:
                    if u == 0:
                        for n in range(F_QT, F_END):
                            pe.wait_ge(side_read[n % 4], seen(n) + 2)
                    mm(ps_s[:, b, 0:N], qaT[:, h, t], kaT[:, h, 0:N], start=True, stop=False)
                    if u == 0:
                        pe.wait_ge(kaT_swapped, 16 * A_HEADS)
                    ins = mm(ps_s[:, b, 0:N], qaT[:, h, t], kaT_swap[:, h, 0:N], start=False, stop=True)
                else:
                    if u == NU_A:
                        for p in range(4):
                            pe.wait_ge(acc_read[p], ACC_LAST[p])
                        pe.wait_ge(kpe_copied, 16)
                    ins = mm(ps_s[:, b, 0:N], qbT[:, h, t], kbT[:, h, 0:N], start=True, stop=True)
                ins.then_inc(scores_ready, 1)

            for u in range(2):
                scores(u)
            wait_chunk(C_UKV)
            for p in range(4):
                pe.wait_ge(acc_read[p], seen(A_KN + p))
                s, cols = C_UKN % RING, slice(p * P, (p + 1) * P)
                products(acc[:, p], ((w_hi[:, s, cols], latT_hi[:, QL_T, :]), (w_hi[:, s, cols], latT_lo[:, QL_T, :]),
                                     (w_lo[:, s, cols], latT_hi[:, QL_T, :])), True, True).then_inc(acc_ready, 1)
            def qpe_transposes():
                pe.wait_ge(qpe_rotated, 2 * TT)
                for quad in range(2):
                    pe.wait_ge(acc_read[2 + quad], seen(A_QPET + quad))
                    for m in range(TT):
                        ins = nc.tensor.transpose(ps_y[:, quad, m * P:(m + 1) * P], qpe_tok[:, m, quad * P:(quad + 1) * P], ident[:, :])
                    ins.then_inc(acc_ready, 1)

            def kpe_transposes():
                pe.wait_ge(kpe_rotated, TT)
                pe.wait_ge(acc_read[2], seen(A_KPET))
                for m in range(TT):
                    ins = nc.tensor.transpose(ps_y[0:ROPE_D, 0, m * P:(m + 1) * P], kpe_tok[:, m, :], ident[:, :])
                ins.then_inc(acc_ready, 1)
            for m in range(TT):
                pe.wait_ge(acc_read[m], seen(A_VB + m))
                s, t0 = C_UKV % RING, slice(m * P, (m + 1) * P)
                products(acc[:, m], ((latT_hi[:, QL_T, t0], w_hi[:, s, :]), (latT_hi[:, QL_T, t0], w_lo[:, s, :]),
                                     (latT_lo[:, QL_T, t0], w_hi[:, s, :])), True, True).then_inc(acc_ready, 1)

            def slot(n):
                if n < 2:
                    pe.wait_ge(side_read[2 + n], SIDE_LAST[2 + n])
                elif not isinstance(slots[n - 2], int):
                    i, b = slots[n - 2]
                    pe.wait_ge(*((oT_lo_ready, 2 * i + 1), (obT_ready, i + 1))[b])
                elif slots[n - 2] < NU_A:
                    pe.wait_ge(probsT_copied, slots[n - 2] + 1)
                else:
                    pe.wait_ge(probsT_lo_ready, slots[n - 2] - NU_A + 1)
                return ps_pT[:, n % 2]

            def transposes(u):
                v, m, h, N = unit(u)
                bank = slot(slot_of[u])
                pe.wait_ge(probs_ready, u + 1)
                for j in range(m + 1):
                    ins = nc.tensor.transpose(bank[:, j * P:(j + 1) * P], probs[:, u % NPROBS, j * P:(j + 1) * P], ident[:, :])
                ins.then_inc(transposed, 1)

            def outputs(u):
                v, m, h, N = unit(u)
                if v < TT:
                    if h == 0:
                        if v < 2:
                            pe.wait_ge(acc_read[v], ACC_LAST[v])
                        else:
                            pe.wait_ge(o_ps_read, v - 1)
                        if v == 0:
                            for t in range(TT):
                                wait_tok(pe, G_V, t)
                    pe.wait_ge(probsT_copied, u + 1)
                    for j in range(m + 1):
                        ins = mm(ps_o[:, v % 2, h * A_DIM:(h + 1) * A_DIM], probsT[:, u % 3, j * P:(j + 1) * P],
                                 va[:, j, h * A_DIM:(h + 1) * A_DIM], start=(j == 0), stop=(j == m))
                    ins.then_inc(pv_done, 1)
                    return
                g, a = divmod(u - NU_A, 2)
                if a == 0:
                    if g < 2:
                        pe.wait_ge(o_ps_read, TT - 1 + g)
                    else:
                        pe.wait_ge(pair_read, g - 1)
                    if g == 0:
                        pe.wait_ge(vb_lo_dve, 2)
                        pe.wait_ge(vb_lo_pool, 2)
                pe.wait_ge(probsT_lo_ready, u - NU_A + 1)
                for j in range(m + 1):
                    ins = mm(ps_o[:, g % 2, 2 * P * a:2 * P * (a + 1)],
                             vb_parts[j][:, h // 2, 2 * a:2 * a + 2].rearrange("p a d -> p (a d)"),
                             probsT_b[:, u % 3, :, j * P:(j + 1) * P], start=(j == 0), stop=(j == m))
                ins.then_inc(pv_done, 1)

            def o_transposes(i, b):
                m = ORDER[i]
                bank = slot(slot_of[i, b])
                if b == 0:
                    pe.wait_ge(o_ready, i + 1)
                else:
                    pe.wait_ge(gate_scaled, i + 1)
                for j in range(4):
                    ins = nc.tensor.transpose(bank[:, j * P:(j + 1) * P], gate[:, m, (4 * b + j) * P:(4 * b + j + 1) * P], ident[:, :])
                ins.then_inc(transposed, 1)

            def out_products(i, a, z):
                last = i == TT - 1
                for n in range(a, z):
                    b, r = divmod(n, 3 * KT)
                    k, j = divmod(r, 3)
                    cols = PIECES[i][b]
                    half, wcols = cols.start // BANK, slice(cols.start % BANK, cols.start % BANK + cols.stop - cols.start)
                    if b == 0 and j == 0 and k in (0, KT // 2):
                        pe.wait_ge(oT_hi_ready, 2 * i + 1 + (k > 0))
                        pe.wait_ge(oT_lo_ready, 2 * i + 1 + (k > 0))
                    if n == 0:
                        if i == 0:
                            pe.wait_ge(w_lo_ready, C_OUT + 2 * KT)
                    if r == 0:
                        if last:
                            if b < 2:
                                pe.wait_ge(masked_ready, NU)
                            else:
                                pe.wait_ge(pair_read, NPAIR - 1)
                        elif i == 0:
                            pe.wait_ge(acc_read[2 + b], ACC_LAST[2 + b])
                        else:
                            pe.wait_ge(out_ps_read, 2 * i - 1 + b)
                    o, w = ((0, wo_hi[:, k, half]), (0, wo_lo(k, half)), (1, wo_hi[:, k, half]))[j]
                    ins = mm(out_ps(i, b), oT[i % 2][:, o, k, :], w[:, wcols], start=(r == 0), stop=(r == 3 * KT - 1))
                    if r == 3 * KT - 1:
                        ins.then_inc(out_ps_ready, 1)

            oT = (oT0, oT1)
            NSTEP = 6 * KT
            per = NSTEP // HEADS
            for u in range(NU + PV_LAG):
                if 2 <= u < NU:
                    scores(u)
                if 0 <= u - T_LAG < NU:
                    transposes(u - T_LAG)
                if u - PV_LAG >= 0:
                    outputs(u - PV_LAG)
                if u == PET_AT:
                    qpe_transposes()
                if u == PET_AT + 6:
                    kpe_transposes()
                i, j = divmod(u - NU_A, HEADS)
                if 0 < i < TT and OT_AT <= j < OT_AT + 2:
                    o_transposes(i - 1, j - OT_AT)
                for t in range(TT - 1):
                    if 0 <= u - OUT_AT[t] < HEADS:
                        out_products(t, per * (u - OUT_AT[t]), per * (u - OUT_AT[t] + 1))
            done = per * (NU + PV_LAG - OUT_AT[TT - 2])
            out_products(TT - 2, done, NSTEP - LAST_STEPS)
            for b in range(2):
                o_transposes(TT - 1, b)
            out_products(TT - 2, NSTEP - LAST_STEPS, NSTEP)
            out_products(TT - 1, 0, 3 * KT * len(PIECES[TT - 1]))


LAST_STEPS = 12
NWARM = 9
T_LAG, PV_LAG = 2, 4
NPROBS = 4
OT_AT = 5
QT_AT, KT_AT = 4, 4
PET_AT = 8
WO_EARLY, WO_LATE = 12, 38
POOL_PAIRS = 8
SCALE_AT = 12
VB_EARLY = 20
Q_ROTATE_AT = [28, 33, 38, 43]


def kernel(**inputs):
    import concourse.bacc as bacc
    from concourse.bass_utils import run_bass_kernel_spmd

    nc = bacc.Bacc("TRN2", target_bir_lowering=False, num_devices=1)
    a = {n: np.asarray(v) for n, v in inputs.items()}
    uq = a["w_uq"][0].reshape(Q_LORA, B_HEADS, B_QK)
    ukv = a["w_ukv"][0].reshape(KV_LORA, B_HEADS, NOPE + V_DIM)

    def parts(w, n):
        return np.concatenate([w[:, :, :n].reshape(w.shape[0], -1), w[:, :, n:].reshape(w.shape[0], -1)], axis=1)

    freqs = np.concatenate([np.float32(10000.0) ** (-np.arange(0, d, 2, dtype=np.float32) / np.float32(d))
                            for d in (A_DIM, ROPE_D)]).astype(np.float32)
    arrays = {
        "x": a["x"][0],
        "xT": a["x"][0].T,
        "positions": a["positions"][0].reshape(TT, P).T,
        "freqs": np.tile(freqs, (P, 1)),
        "w_in": a["w_in"][0],
        "q_norm_g": a["q_norm_g"][0].reshape(QL_T, P).T,
        "w_uq": parts(uq, NOPE),
        "kv_norm_g": a["kv_norm_g"][0].reshape(1, P).T,
        "w_ukv": parts(ukv, NOPE),
        "w_out": a["w_out"][0],
        "ln_g": a["ln_g"],
        "ln_b": a["ln_b"],
    }
    arrays = {n: np.ascontiguousarray(v) for n, v in arrays.items()}
    aps = {n: nc.dram_tensor(f"in_{n}", v.shape, mybir.dt.from_np(v.dtype), kind="ExternalInput").ap()
           for n, v in arrays.items()}
    out = nc.dram_tensor("out_y", (SEQ, D_MODEL), mybir.dt.float32, kind="ExternalOutput").ap()
    build(nc, out=out, **aps)
    r = run_bass_kernel_spmd(nc, [{f"in_{n}": v for n, v in arrays.items()}], core_ids=[0])
    return r.results[0]["out_y"].reshape(1, SEQ, D_MODEL)
```
